# Optimizing a Trainium2 kernel written in Bass

```python
import math
import jax, jax.numpy as jnp
from jax import lax
import numpy as np

D_MODEL = 1024
BATCH = 1
SEQ = 512
DEPTH = 2

MEM_LEN = 256
EPS = 1e-6
Q_BLOCK = 128

A_HEADS = 8
A_QK_DIM = 64
A_V_DIM = 2 * A_QK_DIM
A_WIDTH = A_HEADS * A_V_DIM
B_WIDTH = D_MODEL // 2
CONV_W = 3
C_HEADS = 12
C_DIM = 128
C_WIDTH = C_HEADS * C_DIM
X_HEADS = 4
X_DIM = 128
X_WIDTH = X_HEADS * X_DIM

EVEN_MIX = A_WIDTH + B_WIDTH + X_WIDTH
ODD_MIX = C_WIDTH + X_WIDTH
EVEN_IN = 4 * A_WIDTH + 4 * B_WIDTH + 2 * X_WIDTH
ODD_IN = 4 * C_WIDTH + C_HEADS + 2 * X_WIDTH


def rms_norm(x, g):
    xf = x.astype(jnp.float32)
    y = xf * lax.rsqrt(jnp.mean(xf * xf, axis=-1, keepdims=True) + EPS)
    return (y * g.astype(jnp.float32)).astype(x.dtype)

def alibi_slopes(n_heads):
    return jnp.asarray(np.array([2.0 ** (-8.0 * (i + 1) / n_heads) for i in range(n_heads)], dtype=np.float32))

def sweep_query_blocks(block_fn, *q_arrays):
    seq = q_arrays[0].shape[2]
    nb = seq // Q_BLOCK

    def split(a):
        a = a.reshape(a.shape[:2] + (nb, Q_BLOCK) + a.shape[3:])
        return jnp.moveaxis(a, 2, 0)

    starts = jnp.arange(nb, dtype=jnp.int32) * Q_BLOCK
    out = lax.map(lambda args: block_fn(args[0], *args[1:]), (starts,) + tuple(split(a) for a in q_arrays))
    out = jnp.moveaxis(out, 0, 2)
    return out.reshape(out.shape[:2] + (seq,) + out.shape[4:])

def differential_attention(q, k, v, q_g, k_g, lam_params, out_g, lam_init):
    bsz, seq, _ = q.shape
    q = rms_norm(q.reshape(bsz, seq, A_HEADS, 2, A_QK_DIM), q_g).transpose(0, 2, 3, 1, 4)
    k = rms_norm(k.reshape(bsz, seq, A_HEADS, 2, A_QK_DIM), k_g).transpose(0, 2, 3, 1, 4)
    v = v.reshape(bsz, seq, A_HEADS, A_V_DIM).transpose(0, 2, 1, 3)
    lp = lam_params.astype(jnp.float32)
    lam = jnp.exp(jnp.sum(lp[0] * lp[1])) - jnp.exp(jnp.sum(lp[2] * lp[3])) + lam_init
    slopes = alibi_slopes(A_HEADS)
    scale = A_QK_DIM ** -0.5
    k1, k2 = k[:, :, 0], k[:, :, 1]
    k_pos = jnp.arange(seq, dtype=jnp.int32)

    def block(start, q1b, q2b):
        q_pos = start + jnp.arange(Q_BLOCK, dtype=jnp.int32)
        dist = q_pos[:, None] - k_pos[None, :]
        causal = dist >= 0
        bias = -slopes[:, None, None] * dist.astype(jnp.float32)
        s1 = jnp.einsum('bhqd,bhkd->bhqk', q1b, k1).astype(jnp.float32) * scale + bias
        s2 = jnp.einsum('bhqd,bhkd->bhqk', q2b, k2).astype(jnp.float32) * scale + bias
        p1 = jax.nn.softmax(jnp.where(causal, s1, -jnp.inf), axis=-1)
        p2 = jax.nn.softmax(jnp.where(causal, s2, -jnp.inf), axis=-1)
        attn = (p1 - lam * p2).astype(v.dtype)
        return jnp.einsum('bhqk,bhkd->bhqd', attn, v)

    o = sweep_query_blocks(block, q[:, :, 0], q[:, :, 1])
    o = rms_norm(o, out_g) * (1.0 - lam_init)
    return o.transpose(0, 2, 1, 3).reshape(bsz, seq, A_WIDTH)

def causal_depthwise_conv(u, w, b):
    c = u.shape[-1]
    y = lax.conv_general_dilated(u, w[:, None, :].astype(u.dtype), window_strides=(1,),
                                 padding=[(CONV_W - 1, 0)],
                                 dimension_numbers=('NWC', 'WIO', 'NWC'),
                                 feature_group_count=c)
    return y + b.astype(u.dtype)

def short_gated_conv(h, c_gate, b_gate, w, b):
    return b_gate * causal_depthwise_conv(c_gate * h, w, b)

def forgetting_attention(q, k, v, f_logit, f_bias, q_g, k_g):
    bsz, seq, _ = q.shape
    q = rms_norm(q.reshape(bsz, seq, C_HEADS, C_DIM), q_g).transpose(0, 2, 1, 3)
    k = rms_norm(k.reshape(bsz, seq, C_HEADS, C_DIM), k_g).transpose(0, 2, 1, 3)
    v = v.reshape(bsz, seq, C_HEADS, C_DIM).transpose(0, 2, 1, 3)
    log_f = jax.nn.log_sigmoid(f_logit.astype(jnp.float32) + f_bias.astype(jnp.float32))
    cum = jnp.cumsum(log_f, axis=1).transpose(0, 2, 1)
    scale = C_DIM ** -0.5
    k_pos = jnp.arange(seq, dtype=jnp.int32)

    def block(start, qb, cqb):
        q_pos = start + jnp.arange(Q_BLOCK, dtype=jnp.int32)
        causal = q_pos[:, None] >= k_pos[None, :]
        s = jnp.einsum('bhqd,bhkd->bhqk', qb, k).astype(jnp.float32) * scale
        s = s + (cqb[..., :, None] - cum[:, :, None, :])
        p = jax.nn.softmax(jnp.where(causal, s, -jnp.inf), axis=-1).astype(v.dtype)
        return jnp.einsum('bhqk,bhkd->bhqd', p, v)

    o = sweep_query_blocks(block, q, cum)
    return o.transpose(0, 2, 1, 3).reshape(bsz, seq, C_WIDTH)

def memory_cross_attention(q, mem, mem_g, w_mem_kv, q_g, k_g):
    bsz, seq, _ = q.shape
    m = mem.shape[1]
    mk, mv = jnp.split(rms_norm(mem, mem_g) @ w_mem_kv, 2, axis=-1)
    q = rms_norm(q.reshape(bsz, seq, X_HEADS, X_DIM), q_g)
    mk = rms_norm(mk.reshape(bsz, m, X_HEADS, X_DIM), k_g)
    mv = mv.reshape(bsz, m, X_HEADS, X_DIM)
    s = jnp.einsum('bshd,bmhd->bhsm', q, mk).astype(jnp.float32) * (X_DIM ** -0.5)
    p = jax.nn.softmax(s, axis=-1).astype(mv.dtype)
    o = jnp.einsum('bhsm,bmhd->bshd', p, mv)
    return o.reshape(bsz, seq, X_WIDTH)

def even_layer(h, mem, layer, norm_g, w_in, w_out, a_qn, a_kn, a_lam, a_on,
               b_cw, b_cb, x_qn, x_kn, mem_g, w_mem_kv):
    u = rms_norm(h, norm_g)
    proj = u @ w_in
    cuts = np.cumsum([A_WIDTH] * 4 + [B_WIDTH] * 4 + [X_WIDTH] * 2)[:-1].tolist()
    aq, ak, av, az, bh, bc, bb, bz, xq, xz = jnp.split(proj, cuts, axis=-1)
    lam_init = 0.8 - 0.6 * math.exp(-0.3 * layer)
    ya = differential_attention(aq, ak, av, a_qn, a_kn, a_lam, a_on, lam_init)
    yb = short_gated_conv(bh, bc, bb, b_cw, b_cb)
    yx = memory_cross_attention(xq, mem, mem_g, w_mem_kv, x_qn, x_kn)
    y = jnp.concatenate([ya * jax.nn.silu(az), yb * jax.nn.silu(bz), yx * jax.nn.silu(xz)], axis=-1)
    return h + y @ w_out

def odd_layer(h, mem, norm_g, w_in, w_out, c_qn, c_kn, c_fb, x_qn, x_kn, mem_g, w_mem_kv):
    u = rms_norm(h, norm_g)
    proj = u @ w_in
    cuts = np.cumsum([C_WIDTH] * 4 + [C_HEADS] + [X_WIDTH] * 2)[:-1].tolist()
    cq, ck, cv, cz, cf, xq, xz = jnp.split(proj, cuts, axis=-1)
    yc = forgetting_attention(cq, ck, cv, cf, c_fb, c_qn, c_kn)
    yx = memory_cross_attention(xq, mem, mem_g, w_mem_kv, x_qn, x_kn)
    y = jnp.concatenate([yc * jax.nn.silu(cz), yx * jax.nn.silu(xz)], axis=-1)
    return h + y @ w_out

def first_inputs(seed: int = 0) -> dict:
    key = jax.random.key(seed)
    ks = jax.random.split(key, 32)
    it = iter(range(32))
    ne = (DEPTH + 1) // 2
    no = DEPTH // 2

    def nrm(shape, scale):
        return scale * jax.random.normal(ks[next(it)], shape, jnp.float32)

    def gain(shape):
        return 1.0 + 0.02 * jax.random.normal(ks[next(it)], shape, jnp.float32)

    return {
        "x": nrm((BATCH, SEQ, D_MODEL), 1.0),
        "mem": nrm((BATCH, MEM_LEN, D_MODEL), 1.0),
        "e_norm_g": gain((ne, D_MODEL)),
        "e_w_in": nrm((ne, D_MODEL, EVEN_IN), D_MODEL ** -0.5),
        "e_w_out": nrm((ne, EVEN_MIX, D_MODEL), EVEN_MIX ** -0.5),
        "e_a_q_norm_g": gain((ne, A_QK_DIM)),
        "e_a_k_norm_g": gain((ne, A_QK_DIM)),
        "e_a_lambda": nrm((ne, 4, A_QK_DIM), 0.1),
        "e_a_out_norm_g": gain((ne, A_V_DIM)),
        "e_b_conv_w": nrm((ne, CONV_W, B_WIDTH), CONV_W ** -0.5),
        "e_b_conv_b": nrm((ne, B_WIDTH), 0.02),
        "e_x_q_norm_g": gain((ne, X_DIM)),
        "e_x_k_norm_g": gain((ne, X_DIM)),
        "e_mem_norm_g": gain((ne, D_MODEL)),
        "e_w_mem_kv": nrm((ne, D_MODEL, 2 * X_WIDTH), D_MODEL ** -0.5),
        "o_norm_g": gain((no, D_MODEL)),
        "o_w_in": nrm((no, D_MODEL, ODD_IN), D_MODEL ** -0.5),
        "o_w_out": nrm((no, ODD_MIX, D_MODEL), ODD_MIX ** -0.5),
        "o_c_q_norm_g": gain((no, C_DIM)),
        "o_c_k_norm_g": gain((no, C_DIM)),
        "o_c_forget_b": 3.0 + nrm((no, C_HEADS), 0.5),
        "o_x_q_norm_g": gain((no, X_DIM)),
        "o_x_k_norm_g": gain((no, X_DIM)),
        "o_mem_norm_g": gain((no, D_MODEL)),
        "o_w_mem_kv": nrm((no, D_MODEL, 2 * X_WIDTH), D_MODEL ** -0.5),
    }

def first_block(x, mem, e_norm_g, e_w_in, e_w_out, e_a_q_norm_g, e_a_k_norm_g, e_a_lambda,
              e_a_out_norm_g, e_b_conv_w, e_b_conv_b, e_x_q_norm_g, e_x_k_norm_g,
              e_mem_norm_g, e_w_mem_kv, o_norm_g, o_w_in, o_w_out, o_c_q_norm_g,
              o_c_k_norm_g, o_c_forget_b, o_x_q_norm_g, o_x_k_norm_g, o_mem_norm_g,
              o_w_mem_kv):
    h = x
    for layer in range(DEPTH):
        i = layer // 2
        if layer % 2 == 0:
            h = even_layer(h, mem, layer, e_norm_g[i], e_w_in[i], e_w_out[i],
                           e_a_q_norm_g[i], e_a_k_norm_g[i], e_a_lambda[i], e_a_out_norm_g[i],
                           e_b_conv_w[i], e_b_conv_b[i], e_x_q_norm_g[i], e_x_k_norm_g[i],
                           e_mem_norm_g[i], e_w_mem_kv[i])
        else:
            h = odd_layer(h, mem, o_norm_g[i], o_w_in[i], o_w_out[i],
                          o_c_q_norm_g[i], o_c_k_norm_g[i], o_c_forget_b[i],
                          o_x_q_norm_g[i], o_x_k_norm_g[i], o_mem_norm_g[i], o_w_mem_kv[i])
    return h


CHUNK = 64
N_A_LAYERS = DEPTH // 2
N_B_LAYERS = DEPTH - N_A_LAYERS
SSM_GROUP = 16
N_GROUPS = D_MODEL // SSM_GROUP
SSM_STATE = 64
HEAD_DIM = 64
N_HEADS = D_MODEL // HEAD_DIM
D_FF = 2816
DT_MIN = 1e-3
DT_MAX = 1e-1


def rms_norm_2(x, g):
    xf = x.astype(jnp.float32)
    y = xf * lax.rsqrt(jnp.mean(xf * xf, axis=-1, keepdims=True) + EPS)
    return (y * g.astype(jnp.float32)).astype(x.dtype)

def s5_mixer(xn, w_in, lam_re, lam_im, b_re, b_im, c_re, c_im, d_skip, log_dt, w_glu):
    f32 = jnp.float32
    bsz, seq, _ = xn.shape
    u = (xn @ w_in).astype(f32)
    lam = lax.complex(lam_re.astype(f32), lam_im.astype(f32))
    dt = jnp.exp(log_dt.astype(f32))[:, None]
    a_bar = jnp.exp(lam * dt)
    b_mat = lax.complex(b_re.astype(f32), b_im.astype(f32))
    b_bar = ((a_bar - 1.0) / lam)[..., None] * b_mat
    c_mat = lax.complex(c_re.astype(f32), c_im.astype(f32))
    n_chunks = seq // CHUNK
    u_c = u.reshape(bsz, n_chunks, CHUNK, N_GROUPS, SSM_GROUP).transpose(1, 2, 0, 3, 4)
    a_elems = jnp.broadcast_to(a_bar, (CHUNK, 1, N_GROUPS, SSM_STATE))

    def binop(left, right):
        a_l, b_l = left
        a_r, b_r = right
        return a_r * a_l, a_r * b_l + b_r

    def chunk_step(h0, u_t):
        bu = jnp.einsum('tbgh,gph->tbgp', u_t.astype(jnp.complex64), b_bar)
        a_cum, s = lax.associative_scan(binop, (a_elems, bu), axis=0)
        s = s + a_cum * h0[None]
        y = jnp.einsum('tbgp,ghp->tbgh', s, c_mat).real
        return s[-1], y

    h0 = jnp.zeros((bsz, N_GROUPS, SSM_STATE), jnp.complex64)
    _, y = lax.scan(chunk_step, h0, u_c)
    y = y.transpose(2, 0, 1, 3, 4).reshape(bsz, seq, D_MODEL)
    y = y + d_skip.astype(f32) * u
    g = jax.nn.gelu(y).astype(xn.dtype)
    val, gate = jnp.split(g @ w_glu, 2, axis=-1)
    return val * jax.nn.sigmoid(gate)

def shared_kv(h, kv_norm, w_kv, k_norm):
    bsz, seq, _ = h.shape
    k, v = jnp.split(rms_norm_2(h, kv_norm) @ w_kv, 2, axis=-1)
    k = rms_norm_2(k.reshape(bsz, seq, N_HEADS, HEAD_DIM), k_norm)
    v = v.reshape(bsz, seq, N_HEADS, HEAD_DIM)
    return k, v

def stick_breaking_attention(q, k, v):
    seq = q.shape[1]
    scale = HEAD_DIM ** -0.5
    outs = []
    for i in range(seq // Q_BLOCK):
        q0 = i * Q_BLOCK
        kv_len = q0 + Q_BLOCK
        z = jnp.einsum('bqhd,bkhd->bhqk', q[:, q0:kv_len], k[:, :kv_len]).astype(jnp.float32) * scale
        q_pos = q0 + jnp.arange(Q_BLOCK)[:, None]
        k_pos = jnp.arange(kv_len)[None, :]
        causal = k_pos < q_pos
        log_beta = jax.nn.log_sigmoid(z)
        log_1m = jnp.where(causal, log_beta - z, 0.0)
        later = lax.cumsum(log_1m, axis=3, reverse=True) - log_1m
        w = jnp.where(causal, jnp.exp(log_beta + later), 0.0)
        outs.append(jnp.einsum('bhqk,bkhd->bqhd', w.astype(v.dtype), v[:, :kv_len]))
    return jnp.concatenate(outs, axis=1)

def sb_mixer(xn, w_q, q_norm, k, v, w_o):
    bsz, seq, _ = xn.shape
    q = rms_norm_2((xn @ w_q).reshape(bsz, seq, N_HEADS, HEAD_DIM), q_norm)
    o = stick_breaking_attention(q, k, v)
    return o.reshape(bsz, seq, D_MODEL) @ w_o

def conv_ffn(xn, w_up, conv_w, conv_b, w_down):
    seq = xn.shape[1]
    val, gate = jnp.split(xn @ w_up, 2, axis=-1)
    gp = jnp.pad(gate, ((0, 0), (CONV_W - 1, 0), (0, 0)))
    gc = conv_b + conv_w[0] * gp[:, 0:seq]
    for j in range(1, CONV_W):
        gc = gc + conv_w[j] * gp[:, j:j + seq]
    return (jax.nn.silu(gc) * val) @ w_down

def second_inputs(seed: int = 0) -> dict:
    key = jax.random.key(seed)
    ks = iter(jax.random.split(key, 32))

    def nrm(shape, scale):
        return scale * jax.random.normal(next(ks), shape, jnp.float32)

    def gain(shape):
        return 1.0 + nrm(shape, 0.02)

    d, f = D_MODEL, D_FF
    na, nb = N_A_LAYERS, N_B_LAYERS
    G, P, H = N_GROUPS, SSM_STATE, SSM_GROUP
    n_idx = jnp.arange(P, dtype=jnp.float32)
    x = nrm((BATCH, SEQ, d), 1.0)
    a_norm = gain((na, d))
    a_w_in = nrm((na, d, d), d ** -0.5)
    a_lam_re = -0.5 + nrm((na, G, P), 0.01)
    a_lam_im = math.pi * n_idx + nrm((na, G, P), 0.01)
    a_b_re = nrm((na, G, P, H), (2 * H) ** -0.5)
    a_b_im = nrm((na, G, P, H), (2 * H) ** -0.5)
    a_c_re = nrm((na, G, H, P), P ** -0.5)
    a_c_im = nrm((na, G, H, P), P ** -0.5)
    a_d = nrm((na, d), 1.0)
    a_log_dt = jax.random.uniform(next(ks), (na, G), jnp.float32, math.log(DT_MIN), math.log(DT_MAX))
    a_w_glu = nrm((na, d, 2 * d), d ** -0.5)
    kv_norm = gain((d,))
    w_kv = nrm((d, 2 * d), d ** -0.5)
    k_norm = gain((HEAD_DIM,))
    b_norm = gain((nb, d))
    b_w_q = nrm((nb, d, d), d ** -0.5)
    b_q_norm = gain((nb, HEAD_DIM))
    b_w_o = nrm((nb, d, d), d ** -0.5)
    ffn_norm = gain((DEPTH, d))
    ffn_w_up = nrm((DEPTH, d, 2 * f), d ** -0.5)
    ffn_conv_w = nrm((DEPTH, CONV_W, f), CONV_W ** -0.5)
    ffn_conv_b = nrm((DEPTH, f), 0.02)
    ffn_w_down = nrm((DEPTH, f, d), f ** -0.5)
    return {"x": x, "a_norm": a_norm, "a_w_in": a_w_in, "a_lam_re": a_lam_re, "a_lam_im": a_lam_im,
            "a_b_re": a_b_re, "a_b_im": a_b_im, "a_c_re": a_c_re, "a_c_im": a_c_im, "a_d": a_d,
            "a_log_dt": a_log_dt, "a_w_glu": a_w_glu, "kv_norm": kv_norm, "w_kv": w_kv, "k_norm": k_norm,
            "b_norm": b_norm, "b_w_q": b_w_q, "b_q_norm": b_q_norm, "b_w_o": b_w_o,
            "ffn_norm": ffn_norm, "ffn_w_up": ffn_w_up, "ffn_conv_w": ffn_conv_w,
            "ffn_conv_b": ffn_conv_b, "ffn_w_down": ffn_w_down}

def second_block(x, a_norm, a_w_in, a_lam_re, a_lam_im, a_b_re, a_b_im, a_c_re, a_c_im, a_d,
              a_log_dt, a_w_glu, kv_norm, w_kv, k_norm, b_norm, b_w_q, b_q_norm, b_w_o,
              ffn_norm, ffn_w_up, ffn_conv_w, ffn_conv_b, ffn_w_down):
    h = x
    k = None
    v = None
    for layer in range(DEPTH):
        if layer < N_A_LAYERS:
            i = layer
            h = h + s5_mixer(rms_norm_2(h, a_norm[i]), a_w_in[i], a_lam_re[i], a_lam_im[i],
                             a_b_re[i], a_b_im[i], a_c_re[i], a_c_im[i], a_d[i], a_log_dt[i], a_w_glu[i])
        else:
            j = layer - N_A_LAYERS
            if j == 0:
                k, v = shared_kv(h, kv_norm, w_kv, k_norm)
            h = h + sb_mixer(rms_norm_2(h, b_norm[j]), b_w_q[j], b_q_norm[j], k, v, b_w_o[j])
        h = h + conv_ffn(rms_norm_2(h, ffn_norm[layer]), ffn_w_up[layer], ffn_conv_w[layer],
                         ffn_conv_b[layer], ffn_w_down[layer])
    return h


def setup_inputs(seed=0):
    out = dict(first_inputs(seed))
    for name, value in second_inputs(seed + 1).items():
        if name != "x":
            out[name + "_2"] = value
    return out


def reference(
    x, mem, e_norm_g, e_w_in, e_w_out, e_a_q_norm_g, e_a_k_norm_g, e_a_lambda, e_a_out_norm_g,
    e_b_conv_w, e_b_conv_b, e_x_q_norm_g, e_x_k_norm_g, e_mem_norm_g, e_w_mem_kv, o_norm_g,
    o_w_in, o_w_out, o_c_q_norm_g, o_c_k_norm_g, o_c_forget_b, o_x_q_norm_g, o_x_k_norm_g,
    o_mem_norm_g, o_w_mem_kv, a_norm_2, a_w_in_2, a_lam_re_2, a_lam_im_2, a_b_re_2, a_b_im_2,
    a_c_re_2, a_c_im_2, a_d_2, a_log_dt_2, a_w_glu_2, kv_norm_2, w_kv_2, k_norm_2, b_norm_2,
    b_w_q_2, b_q_norm_2, b_w_o_2, ffn_norm_2, ffn_w_up_2, ffn_conv_w_2, ffn_conv_b_2,
    ffn_w_down_2,
):
    x = first_block(
        x, mem, e_norm_g, e_w_in, e_w_out, e_a_q_norm_g, e_a_k_norm_g, e_a_lambda,
        e_a_out_norm_g, e_b_conv_w, e_b_conv_b, e_x_q_norm_g, e_x_k_norm_g, e_mem_norm_g,
        e_w_mem_kv, o_norm_g, o_w_in, o_w_out, o_c_q_norm_g, o_c_k_norm_g, o_c_forget_b,
        o_x_q_norm_g, o_x_k_norm_g, o_mem_norm_g, o_w_mem_kv,
    )
    return second_block(
        x, a_norm_2, a_w_in_2, a_lam_re_2, a_lam_im_2, a_b_re_2, a_b_im_2, a_c_re_2, a_c_im_2,
        a_d_2, a_log_dt_2, a_w_glu_2, kv_norm_2, w_kv_2, k_norm_2, b_norm_2, b_w_q_2,
        b_q_norm_2, b_w_o_2, ffn_norm_2, ffn_w_up_2, ffn_conv_w_2, ffn_conv_b_2, ffn_w_down_2,
    )


_drawn_inputs = setup_inputs


def setup_inputs(seed=0):
    import zlib

    import numpy as np

    out = dict(_drawn_inputs(seed))
    spreads = {}
    factors = {'e_norm_g': 2.681,
     'e_a_q_norm_g': 7.533,
     'e_a_k_norm_g': 7.351,
     'e_a_out_norm_g': 6.805,
     'e_b_conv_b': 8.0,
     'e_x_q_norm_g': 8.0,
     'e_x_k_norm_g': 8.0,
     'e_mem_norm_g': 8.0,
     'o_norm_g': 8.0,
     'o_c_q_norm_g': 8.0,
     'o_c_k_norm_g': 8.0,
     'o_x_q_norm_g': 8.0,
     'o_x_k_norm_g': 8.0,
     'o_mem_norm_g': 8.0,
     'a_norm_2': 56.072,
     'a_lam_re_2': 200.0,
     'kv_norm_2': 138.098,
     'k_norm_2': 200.0,
     'b_norm_2': 200.0,
     'b_q_norm_2': 200.0,
     'ffn_norm_2': 24.104,
     'ffn_conv_b_2': 35.752,
     'a_lam_im_2': 64.0,
     'a_b_re_2': 64.0,
     'a_b_im_2': 64.0,
     'a_c_re_2': 64.0,
     'a_c_im_2': 64.0,
     'a_log_dt_2': 64.0}
    for name, (base, spread) in spreads.items():
        noise = np.random.default_rng([zlib.crc32(name.encode()), seed]).standard_normal(out[name].shape)
        drawn = base * np.exp(spread * noise) if base else spread * noise
        out[name] = __import__('jax').numpy.asarray(drawn.astype(out[name].dtype))
    for name, factor in factors.items():
        out[name] = (out[name] * factor).astype(out[name].dtype)
    return out
```

```python
from contextlib import ExitStack

import concourse.bass as bass
from concourse import mybir

F32 = mybir.dt.float32
F32R = mybir.dt.float32r
I32 = mybir.dt.int32
ALU = mybir.AluOpType
ACT = mybir.ActivationFunctionType
AX_X = mybir.AxisListType.X

P = 128
SEQ, DM, MEM = 512, 1024, 256
TT = SEQ // P
KT = DM // P
DFF = 2816
EPS = 1e-6
BIG = -3.0e38
HL = 2
RAW = 2
LAM_INIT = 0.8 - 0.6 * 1.0
A_HEADS, C_HEADS, X_HEADS, SB_HEADS = 8, 12, 4, 16


def weight_units(w):
    units = []

    def cols(mat, k0, kn, c):
        v = mat.rearrange("(k p) n -> p k n", p=P)
        half = kn // 2
        return [(v[:, k0:k0 + half, c:c + 512], slice(0, half), slice(0, 512)),
                (v[:, k0 + half:k0 + kn, c:c + 512], slice(half, kn), slice(0, 512))]

    def paired(mat, k0, ca, cb):
        v = mat.rearrange("(k p) n -> p k n", p=P)
        return [(v[:, k0:k0 + 4, ca:ca + 256], slice(0, 4), slice(0, 256)),
                (v[:, k0:k0 + 4, cb:cb + 256], slice(0, 4), slice(256, 512))]

    def chunk(mat, c):
        units.append(cols(mat, 0, 4, c))
        units.append(cols(mat, 4, 4, c))

    def down(mat, kt):
        for k0 in range(0, kt, 4):
            for c in (0, 512):
                units.append(cols(mat, k0, min(4, kt - k0), c))

    for c in (0, 512):
        chunk(w["e_w_mem_kv"], c)
    for o in (6144, 6656):
        chunk(w["e_w_in"], o)
    for g in range(2):
        for o in (3072, 0, 1024, 2048):
            chunk(w["e_w_in"], o + 512 * g)
    for o in (4096, 4608, 5120, 5632):
        chunk(w["e_w_in"], o)
    down(w["e_w_out"], 16)
    for c in (0, 512):
        chunk(w["o_w_mem_kv"], c)
    for o in (6156, 6668):
        chunk(w["o_w_in"], o)
    for g in range(3):
        for o in (4608, 0, 1536, 3072):
            chunk(w["o_w_in"], o + 512 * g)
    down(w["o_w_out"], 16)
    for c in (0, 512):
        chunk(w["a_w_in"], c)
    for c in range(4):
        for k0 in (0, 4):
            units.append(paired(w["a_w_glu"], k0, 256 * c, DM + 256 * c))
    for layer in range(2):
        if layer == 1:
            for c in range(4):
                chunk(w["w_kv"], 512 * c)
            for c in range(2):
                chunk(w["b_w_q"], 512 * c)
            down(w["b_w_o"], 8)
        for c in range(11):
            for k0 in (0, 4):
                units.append(paired(w["ffn_w_up"][layer], k0, DFF + 256 * c, 256 * c))
        down(w["ffn_w_down"][layer], 22)
    return units


class Stage:

    def __init__(self, kind, src=None, name=None, T=TT, n=0, h=None, y=None, kt=0, c=0, aux=None, kt_ready=None,
                 akind=None, heads=0, y0=0, operand=None, gate=None, us=None, prep=None, owed=None, ev=None,
                 wtype=None, nu=0, to=None, step=1, stage_at=0, hd=0, dst=0, layer=0, host=None, host_at=0):
        self.kind, self.src, self.name, self.T, self.n, self.h, self.y, self.kt = kind, src, name, T, n, h, y, kt
        self.c, self.aux, self.kt_ready, self.akind, self.heads, self.y0 = c, aux, kt_ready, akind, heads, y0
        self.operand, self.gate, self.us, self.prep, self.owed, self.ev = operand, gate, us, prep, owed, ev
        self.wtype, self.nu, self.to, self.step, self.stage_at = wtype, nu, to, step, stage_at
        self.hd, self.dst, self.layer = hd, dst, layer
        self.host, self.host_at = host, host_at


class Counts:

    def __init__(self):
        self.of, self.total, self.given = {}, {}, {}

    def mark(self, *key):
        assert key not in self.of, key
        self.total[key[0]] = self.total.get(key[0], 0) + 1
        self.of[key] = self.total[key[0]]


def build(nc, w, out, upto=None):
    units = weight_units(w)
    NU = len(units)

    with ExitStack() as ctx:
        def sb(name, shape, dt=F32):
            return ctx.enter_context(nc.sbuf_tensor(name, shape, dt))

        def sem(name):
            return ctx.enter_context(nc.semaphore(name))

        h = sb("h", [P, TT, DM])
        u_hi = sb("u_hi", [P, KT, SEQ], F32R)
        u_lo = sb("u_lo", [P, KT, SEQ], F32R)
        raw = sb("raw", [P, RAW, 4, 512])
        w_hi = sb("w_hi", [P, HL, 4, 512], F32R)
        w_lo = sb("w_lo", [P, HL, 4, 512], F32R)
        big = sb("big", [P, 22, SEQ])
        att = sb("att", [P, 24, SEQ])
        work = sb("work", [P, 6, 512])
        junk = work[:, 0:2, :]
        sq = work[:, 2:6, :]
        bias_tile = sb("bias_tile", [P, 512])
        upper = sb("upper", [P, 512])
        ident = sb("ident", [P, P])
        ones = upper[:, P:2 * P]
        below = sb("below", [P, P])
        par = sb("par", [P, 320])
        f_bias = sb("f_bias", [P, C_HEADS])
        small = sb("small", [P, 304])
        G = ctx.enter_context(nc.psum_tensor("G", [P, 4, 512], F32))
        X = ctx.enter_context(nc.psum_tensor("X", [P, 4, 512], F32))

        at, loads, pos = {}, [], 0

        vec = att[:, 0, 0:3 * P].rearrange("p (a b) -> p a b", b=P)

        def tiles(v):
            return v.rearrange("(k p) -> k p", p=P)

        def place(name, src, rows):
            nonlocal pos
            at[name] = pos
            done = 0
            while done < rows:
                k = min(rows - done, P - pos % P)
                loads.append((vec[pos % P:pos % P + k, pos // P, :], src[done:done + k, :]))
                pos += k
                done += k

        for name, v in (("e_norm", w["e_norm_g"]), ("o_norm", w["o_norm_g"]), ("e_mem", w["e_mem_norm_g"]),
                        ("o_mem", w["o_mem_norm_g"]), ("a_norm", w["a_norm"]), ("kv_norm", w["kv_norm"]),
                        ("b_norm", w["b_norm"]), ("ffn0", w["ffn_norm"][0]), ("ffn1", w["ffn_norm"][1]),
                        ("d_skip", w["a_d"])):
            place(name, tiles(v), KT)
        for name, v in (("cq", w["o_c_q_norm_g"]), ("ck", w["o_c_k_norm_g"]), ("exq", w["e_x_q_norm_g"]),
                        ("exk", w["e_x_k_norm_g"]), ("oxq", w["o_x_q_norm_g"]), ("oxk", w["o_x_k_norm_g"]),
                        ("aout", w["e_a_out_norm_g"])):
            place(name, v.rearrange("(o p) -> o p", o=1), 1)
        for name, v in (("aq", w["e_a_q_norm_g"]), ("ak", w["e_a_k_norm_g"]), ("sk", w["k_norm"]),
                        ("sq", w["b_q_norm"])):
            at[name] = pos
            for half in range(2):
                loads.append((vec[pos % P:pos % P + 1, pos // P, 64 * half:64 * half + 64],
                              v.rearrange("(o p) -> o p", o=1)))
            pos += 1
        for j in range(3):
            place(f"e_cw{j}", tiles(w["e_b_conv_w"][j]), 4)
        place("e_cb", tiles(w["e_b_conv_b"]), 4)
        for layer in range(2):
            for j in range(3):
                place(f"f{layer}_cw{j}", tiles(w["ffn_conv_w"][layer][j]), 22)
            place(f"f{layer}_cb", tiles(w["ffn_conv_b"][layer]), 22)
        loads.append((f_bias[:, :], w["o_c_forget_b"].partition_broadcast(P)))
        loads.append((junk[:, 0, 0:256], w["e_a_lambda"].rearrange("a d -> (a d)").partition_broadcast(P)))
        assert 2 * P < pos <= 320, pos

        def gain(name, k=0):
            return par[:, at[name] + k:at[name] + k + 1]

        ss, lnv, rstd = small[:, 0:8], small[:, 8:16], small[:, 16:24]
        neg_lam, lam_t, eps_c, one_c = small[:, 24:25], small[:, 25:29], small[:, 29:30], small[:, 30:31]
        mx, nmx, rs, rr = small[:, 32:36], small[:, 36:40], small[:, 40:44], small[:, 44:48]
        oss, oln, orstd = small[:, 48:52], small[:, 52:56], small[:, 56:60]
        logf = small[:, 64:112]
        wcf = small[:, 112:208]
        qk_ss, qk_t, qk_rstd = small[:, 208:240], small[:, 240:272], small[:, 272:304]
        logt = att[:, 23, 0:48]
        big_mk = big[:, 16:18, :].rearrange("p a (b t) -> p (a b) t", b=2)
        big_mv = big[:, 18:20, :]
        cum = big[0:C_HEADS, 20, :]
        row = big[0:C_HEADS, 21, :]

        counts = Counts()
        mark = counts.mark
        plan = []
        freed = []
        gfreed = [[], [], [], []]
        state = dict(n=0, norm=0, chunk=0)

        def aux(*key, ready=True):
            freed.append(key)
            if ready:
                mark("aux_ready", len(freed) - 1)
            return len(freed) - 1

        def stage(kind, **fields):
            s = Stage(kind, **fields)
            s.i = len(plan)
            plan.append(s)
            return s

        def plan_norm(src, name, T=TT, again=0):
            s = stage("norm", src=src, name=name, T=T, n=state["n"], h=state.get("h"), y=state.get("y"), step=again)
            if not again:
                for t in range(T):
                    mark("squared", s.i, t)
                for t in range(T):
                    mark("xn_ready", s.i, t)
            s.aux = [aux("u_ready", s.i, k) for k in range(KT)]
            for k in range(KT):
                mark("u_hi_done", s.i, k)
                mark("u_ready", s.i, k)
            state["norm"] = s.i
            state["kt_ready"] = [("u_ready", s.i, k) for k in range(KT)]
            return s

        def plan_owed(q, m):
            q.aux = [] if m == 0 else q.aux
            q.aux.append(aux("operand", q.i, m))
            mark("operand", q.i, m)
            state["operand"] = ("operand", q.i, m)

        def plan_finish(q):
            for m in range(q.T):
                mark("summed", q.i, m)
            for m in range(q.T):
                mark("xn_ready", q.i, m)

        def plan_owed_stage(q):
            stage("owed", owed=q)
            plan_finish(q)
            for m in range(q.T):
                plan_owed(q, m)

        def plan_chunks(items, host=None):
            owed = None
            for k, (kind, wtype, f) in enumerate(items):
                q = stage("chunk", **(dict(ev=kind, wtype=wtype, T=TT, nu=2, owed=owed, to=att, step=1, stage_at=0) | f))
                if kind == "memkv":
                    q.T, q.nu = 2, 4
                q.host, q.host_at = host, 8 * k
                q.n = state["n"]
                q.c = state["chunk"]
                state["n"] += q.nu
                state["chunk"] += 1
                q.kt_ready = state["kt_ready"]
                q.y_before = state.get("y")
                if owed is not None:
                    plan_finish(owed)
                for b in range(8):
                    if host is not None:
                        plan_slot(host, q.host_at + b)
                    if b < 4:
                        continue
                    m = b - 4
                    if owed is not None and m < owed.T:
                        plan_owed(owed, m)
                    if kind == "qk" or (kind == "memkv" and m < 2):
                        mark("staged", q.i, m)
                        mark("q_squared", q.i, m)
                        gfreed[m].append(("staged", q.i, m))
                    elif kind == "memkv" or kind == "v":
                        mark("operand", q.i, "v", m)
                        state["operand"] = ("operand", q.i, "v", m)
                        gfreed[m].append(("operand", q.i, "v", m))
                    elif kind in ("silu", "conv_h"):
                        mark("gate", q.i, m)
                        gfreed[m].append(("gate", q.i, m))
                        state["gate"] = ("gate", q.i, m)
                    elif kind in ("conv_c", "conv_b"):
                        mark("conv", q.i, m)
                        gfreed[m].append(("conv", q.i, m))
                    elif kind == "conv_z":
                        mark("gate", q.i, m)
                        gfreed[m].append(("gate", q.i, m))
                        mark("y", q.i, m)
                        state["y"] = ("y", q.i, m)
                    elif kind == "up":
                        if m < 2:
                            mark("conv", q.i, m)
                            gfreed[m].append(("conv", q.i, m))
                            mark("gate", q.i, m)
                        else:
                            mark("y", q.i, m)
                            state["y"] = ("y", q.i, m)
                            gfreed[m].append(("y", q.i, m))
                    elif kind == "glu":
                        mark("gate", q.i, m)
                        mark("h_done", q.i, m)
                        gfreed[m].append(("h_done", q.i, m))
                        state["h"] = ("h_done", q.i, m)
                    elif kind == "s5u":
                        mark("operand", q.i, "v", m)
                        state["operand"] = ("operand", q.i, "v", m)
                        gfreed[m].append(("operand", q.i, "v", m))
                owed = q if kind in ("qk", "memkv") else None
            if host is not None:
                end = stage("attend_rest", host=host, host_at=8 * len(items))
                for t in range(end.host_at, host.slots):
                    plan_slot(host, t)
            return owed

        def is_last(s, t):
            return 0 <= t < len(s.steps) and s.steps[t][1] == TT - 1

        def attention(kind, heads, y0):
            s = Stage("attend", akind=kind, heads=heads, y0=y0, aux={}, operand=state["operand"],
                      gate=state.get("gate"))
            s.i = ("attention", kind, len(plan))
            s.steps = [(hd, i) for hd in range(heads) for i in range(TT)]
            s.slots = len(s.steps) + (5 if kind == "A" else 3)
            return s

        def plan_slot(s, t):
            if t >= s.slots:
                return
            use, kind, T = s.aux, s.akind, len(s.steps)
            if kind == "A" and is_last(s, t - 5):
                use["ot", s.steps[t - 5][0]] = aux("y", s.i, s.steps[t - 5][0])
            if is_last(s, t - 3):
                hd = s.steps[t - 3][0]
                if kind == "A":
                    use["pv", hd] = aux("on_ready", s.i, hd)
                    mark("o_squared", s.i, hd)
                    mark("on_ready", s.i, hd)
                else:
                    use["pv", hd] = aux("y", s.i, hd)
                    mark("y", s.i, hd)
            if kind == "A" and is_last(s, t - 5):
                mark("y", s.i, s.steps[t - 5][0])
            if 0 <= t - 2 < T:
                use["pt", t - 2] = aux("pt_copied", s.i, t - 2)
                mark("pt_copied", s.i, t - 2)
            if t < T:
                for m in range(2 if kind == "A" else 1):
                    use["qk", t, m] = aux(*(("exp_done", s.i, t) if kind == "X" else ("score", s.i, t)))
                mark("score", s.i, t)
                mark("exp_done", s.i, t)
                mark("p_ready", s.i, t)
                if kind == "C" and s.steps[t][1] == 0:
                    mark("row_ready", s.i, s.steps[t][0])
            if t == s.slots - 1:
                state["y"] = ("y", s.i, s.heads - 1)

        def plan_attention(s):
            stage("attend_rest", host=s, host_at=0)
            for t in range(s.slots):
                plan_slot(s, t)

        def plan_sb():
            s = stage("attend", akind="SB", heads=SB_HEADS, aux={}, operand=state["operand"])
            use = s.aux
            s.gfreed = [gfreed[m][-1] for m in range(4)]
            for k in range(-1, s.heads + 3):
                if k + 1 < s.heads:
                    for j in range(TT):
                        use["qk", k + 1, j] = aux("z", s.i, k + 1, j)
                        mark("z", s.i, k + 1, j)
                    mark("log_done", s.i, k + 1)
                if 1 <= k <= s.heads:
                    mark("sp", s.i, k - 1)
                    for j in range(TT):
                        mark("later", s.i, k - 1, j)
                        mark("arg", s.i, k - 1, j)
                if 2 <= k < s.heads + 2:
                    mark("exp_done", s.i, k - 2)
                    use["pv", k - 2] = aux("y", s.i, k - 2)
                    mark("y", s.i, k - 2)
            state["y"] = ("y", s.i, s.heads - 1)

        def plan_down(kt):
            s = stage("down", kt=kt, n=state["n"], c=state["chunk"], y=state["y"])
            s.groups = [range(k, min(k + 4, kt)) for k in range(0, kt, 4)]
            state["n"] += 2 * len(s.groups)
            state["chunk"] += 1
            for k in range(kt):
                mark("u_hi_done", s.i, k)
                mark("u_ready", s.i, k)
            for m in range(4):
                mark("h_done", s.i, 0, m)
                gfreed[m].append(("h_done", s.i, 0, m))
            s.aux = [aux("h_done", s.i, 1, m, ready=False) for m in range(4)]
            for m in range(4):
                mark("h_done", s.i, 1, m)
            state["h"] = ("h_done", s.i, 1, 3)
            return s

        def plan_ffn(layer):
            plan_norm("h", f"ffn{layer}")
            plan_chunks([("up", "T", dict(dst=2 * c, layer=layer)) for c in range(11)])
            plan_down(22)

        def plan_even():
            plan_norm("mem", "e_mem", T=2)
            owed = plan_chunks([("memkv", "mem", dict(name="exk", hd=128))])
            plan_norm("h", "e_norm")
            plan_owed_stage(owed)
            plan_chunks([("qk", "N", dict(name="exq", dst=0, hd=128)), ("silu", "T", dict(dst=12))])
            before = attention("X", X_HEADS, 12)
            for g in range(2):
                plan_chunks([("silu", "T", dict(dst=4 * g)), ("qk", "N", dict(name="aq", dst=0, hd=64)),
                             ("qk", "N", dict(name="ak", dst=4, hd=64)), ("v", "N", dict(dst=8))], host=before)
                before = attention("A", 4, 4 * g)
                before.gate = ("gate", plan[-5].i, 3)
            plan_chunks([("conv_h", "T", {}), ("conv_c", "T", {}), ("conv_b", "T", {}), ("conv_z", "T", dict(dst=8))],
                        host=before)
            plan_down(16)

        def plan_odd():
            plan_norm("mem", "o_mem", T=2)
            owed = plan_chunks([("memkv", "mem", dict(name="oxk", hd=128))])
            plan_norm("h", "o_norm")
            plan_owed_stage(owed)
            s = stage("forget", kt_ready=state["kt_ready"])
            s.aux = []
            for m in range(TT):
                s.aux.append(aux("f_logit", s.i, m))
                mark("f_logit", s.i, m)
            mark("f_log", s.i)
            mark("log_f", s.i)
            s.aux_cum = aux("cum_done", s.i)
            mark("cum_done", s.i)
            plan_chunks([("qk", "N", dict(name="oxq", dst=0, hd=128)), ("silu", "T", dict(dst=12))])
            before = attention("X", X_HEADS, 12)
            for g in range(3):
                plan_chunks([("silu", "T", dict(dst=4 * g)), ("qk", "N", dict(name="cq", dst=0, hd=128)),
                             ("qk", "N", dict(name="ck", dst=4, hd=128)), ("v", "N", dict(dst=8))], host=before)
                before = attention("C", 4, 4 * g)
            plan_attention(before)
            plan_down(16)

        NSUP, NPAIR, NI = SEQ // 8, 32, 8
        attf = att[:, :, :].rearrange("p a b -> p (a b)")
        bigf = big[:, :, :].rearrange("p a b -> p (a b)")
        s5_rows = att[0:NPAIR, 0, 0:384].rearrange("p (a b) -> p a b", a=3)
        s5_ldt = att[0:NPAIR, 1, 0:2]
        s5_crow = [att[:, 2, :], att[:, 3, :]]
        s5_b = [att[:, 4, :], att[:, 5, :]]
        s5_c = [att[:, 6, :], att[:, 7, :]]

        def s5_v(k):
            return att[:, 8, 32 * k:32 * k + 32] if k < 16 else att[:, 9, 32 * (k - 16):32 * (k - 16) + 32]

        s5_pw = attf[:, 10 * 512:10 * 512 + 9 * 64].rearrange("p (t c g) -> p t c g", t=9, c=2)
        s5_bt = [att[:, 20, :], att[:, 21, :]]
        s5_coef = small[:, 64:192].rearrange("p (a c g) -> p a c g", a=2, c=2)

        def s5_zp(i):
            o = 2176 * (i % 2)
            z = bigf[:, o:o + 1152].rearrange("p (c g t h) -> p c g t h", c=2, g=4, h=16)
            pp = bigf[:, o + 1152:o + 2176].rearrange("p (c g t h) -> p c g t h", c=2, g=4, h=16)
            return z, pp, bigf[:, o:o + 1152]

        s5_tmp = bigf[:, 4352:4352 + 576]
        s5_tmp_pool = att[:, 22, :]
        s5_pst = [attf[:, o:o + 1024].rearrange("p (g c n) -> p g c n", g=4, c=2) for o in (12 * 512, 16 * 512)]
        s5_kst = [attf[0:16, o:o + 1024].rearrange("p (g n) -> p g n", g=8) for o in (14 * 512, 18 * 512)]
        dP = nc.dram_tensor("s5_in", (P, NI, 1024), F32).ap()
        dZ = nc.dram_tensor("s5_out", (P, NI, 1152), F32).ap()
        dK = nc.dram_tensor("s5_kernel", (64, 16, P), F32).ap()
        dU = nc.dram_tensor("s5_u", (8, 64, 16, NSUP), F32).ap()
        dY = nc.dram_tensor("s5_y", (8, 64, 16, NSUP), F32).ap()
        s5_u = att[:, 0:8, :].rearrange("p k (t j) -> p k t j", t=8)
        s5_U = att[:, 8:16, :].rearrange("p k (g j) -> p (k g) j", g=8)
        s5_S = attf[:, 16 * 512:24 * 512].rearrange("p (j c g) -> p j c g", j=NSUP, c=2)
        s5_L = bigf[:, 0:8192].rearrange("p (g n) -> p g n", g=64)
        s5_y = big[:, 0:8, :]
        s5_buf2 = bigf[:, 8192 + 2304:8192 + 2304 + 128]

        S5B = 3
        s5_bufs = [bigf[:, 8192:8192 + 1152], bigf[:, 8192 + 1152:8192 + 2304],
                   work[:, :, :].rearrange("p a b -> p (a b)")[:, 1024:1024 + 1152]]

        def s5_buf(n):
            return s5_bufs[n % S5B]

        def s5_on_pool(i):
            return i % 4 != 3

        def plan_s5():
            s = stage("s5prep", y=state.get("y"), h=state.get("h"), n=state["n"])
            s.at_lam = aux("s5_lam", s.i)
            mark("s5_lam", s.i)
            s.at_c = [aux("s5_ct", s.i, c) for c in range(2)]
            for c in range(2):
                mark("s5_ct", s.i, c)
            for name in ("s5_dtrow", "s5_edt", "s5_theta", "s5_sin", "s5_bbar"):
                mark(name, s.i)
            s.pt, s.kk = {}, {}
            for i in range(NI):
                mark("s5_set", s.i, i)
                if s5_on_pool(i):
                    mark("s5_pset", s.i, i)
                for c in range(2):
                    s.pt[i, c] = aux("s5_evac", s.i, i, "p", c)
                    mark("s5_evac", s.i, i, "p", c)
                for k in range(2):
                    s.kk[i, k] = aux("s5_evac", s.i, i, "k", k)
                    mark("s5_evac", s.i, i, "k", k)
            prep = s
            plan_norm("h", "a_norm")
            plan_chunks([("s5u", "T", dict(dst=0)), ("s5u", "T", dict(dst=4))])
            us = [p for p in plan if p.kind == "chunk"][-2:]
            s = stage("s5", us=us, prep=prep)
            s.v = [aux("s5_vdone", s.i, i) for i in range(NI)]
            for i in range(NI):
                mark("s5_vdone", s.i, i)
            mark("s5_scanned", s.i)
            s.yy = [aux("s5_ydone", s.i, i) for i in range(2 * NI)]
            for i in range(2 * NI):
                mark("s5_ydone", s.i, i)
            for k in range(KT):
                mark("s5_skip", s.i, k)
                mark("s5_gelu", s.i, k)
                mark("u_hi_done", s.i, k)
                mark("u_ready", s.i, k)
            state["kt_ready"] = [("u_ready", s.i, k) for k in range(KT)]
            plan_chunks([("glu", "N", dict(dst=256 * c)) for c in range(4)])

        gains = stage("gains", aux=aux("gains", 0))
        mark("gains", 0)
        plan_even()
        plan_odd()
        plan_s5()
        plan_ffn(0)
        plan_norm("h", "kv_norm")
        plan_chunks([("qk", "N", dict(name="sk", dst=8, hd=64, to=big)),
                     ("qk", "N", dict(name="sk", dst=12, hd=64, to=big)),
                     ("v", "N", dict(dst=0, step=2)), ("v", "N", dict(dst=1, step=2))])
        plan_norm("h", "b_norm", again=1)
        plan_owed_stage(plan_chunks([("qk", "N", dict(name="sq", dst=8, hd=64, stage_at=4)),
                                     ("qk", "N", dict(name="sq", dst=12, hd=64, stage_at=4))]))
        plan_sb()
        plan_down(8)
        plan_ffn(1)
        if upto is not None:
            del plan[upto:]

        sems = {name: sem(name) for name in counts.total}
        NUSED = sum(2 * len(s.groups) if s.kind == "down" else s.nu for s in plan)

        def at_(*key):
            return sems[key[0]], counts.of[key]

        def by(*key):
            given = counts.given.get(key[0], 0) + 1
            assert counts.of[key] == given, (key, counts.of[key], given)
            counts.given[key[0]] = given
            return sems[key[0]], 1

        par_loaded = sem("par_loaded")
        h_loaded = sem("h_loaded")
        mem_loaded = sem("mem_loaded")
        raw_loaded = [sem(f"raw_loaded{i}") for i in range(RAW)]
        w_hi_done = sem("w_hi_done")
        w_lo_done = sem("w_lo_done")
        blocks = sem("blocks")
        consts = sem("consts")
        dconsts = sem("dconsts")
        aconsts = sem("aconsts")
        chain = {e: sem(f"{e}_chain") for e in ("act", "dve", "pool")}
        chained = dict(act=0, dve=0, pool=0)
        out_done = sem("out_done")
        s5_loaded = sem("s5_loaded")
        s5_stored = [sem("s5_stored0"), sem("s5_stored1")]
        s5_u_stored = sem("s5_u_stored")
        s5_u_loaded = sem("s5_u_loaded")
        s5_op_loaded = [sem(f"s5_op_loaded{i}") for i in range(S5B)]
        s5_l_zero = sem("s5_l_zero")
        s5_l_loaded = sem("s5_l_loaded")
        s5_y_stored = sem("s5_y_stored")
        s5_y_loaded = sem("s5_y_loaded")

        def link(name, eng, ins):
            chained[name] += 1
            ins.then_inc(chain[name], 1)
            eng.wait_ge(chain[name], chained[name])

        norms = [s for s in plan if s.kind == "norm"]
        s5_preps = [s for s in plan if s.kind == "s5prep"]
        qk_chunks = [s for s in plan if s.kind == "chunk" and s.ev in ("qk", "memkv")]
        mem_norms = [s for s in norms if s.src == "mem"]
        last_h = [s for s in plan if s.kind == "down"][-1]
        last_h = ("h_done", last_h.i, 1, 3)
        mem_view = att[:, 8:12, :].rearrange("p (t a) n -> p t (a n)", t=2)
        xn_view = att[:, 16:24, :].rearrange("p (t a) n -> p t (a n)", t=4)
        block = ctx.enter_context(nc.Block())

        @block.sync
        def _(sp):
            sp.wait_ge(dconsts, 1)
            for dst, src in loads[0::2]:
                sp.dma_start(dst, src).then_inc(par_loaded, 16)
            sp.dma_start(h[:, :, :], w["x"].rearrange("(t p) n -> p t n", p=P)).then_inc(h_loaded, 16)
            sp.dma_start(wcf.rearrange("p (k n) -> p k n", k=KT),
                         w["o_w_in"][:, 6144:6156].rearrange("(k p) n -> p k n", p=P)).then_inc(h_loaded, 16)
            for n in range(NUSED):
                for s in mem_norms[1:]:
                    if s.n - 3 == n:
                        sp.wait_ge(*at_(*s.y))
                        sp.dma_start(att[:, 8:12, :].rearrange("p (t a) n -> p t (a n)", t=2),
                                     w["mem"].rearrange("(t p) n -> p t n", p=P)).then_inc(mem_loaded, 16)
                if n >= RAW:
                    sp.wait_ge(w_hi_done, n - RAW + 1)
                    sp.wait_ge(w_lo_done, n - RAW + 1)
                for src, ks, cs in units[n]:
                    sp.dma_start(raw[:, n % RAW, ks, cs], src).then_inc(raw_loaded[n % RAW], 16)
            sp.wait_ge(*at_(*last_h))
            sp.dma_start(out.rearrange("(t p) n -> p t n", p=P), h[:, :, :]).then_inc(out_done, 16)
            sp.wait_ge(out_done, 16)

        def complex_mul(name, eng, V, dr, di, ar, ai, br, bi, t1, negate_im=False):
            tt = V.tensor_tensor
            link(name, eng, tt(t1, ai, bi, ALU.mult))
            link(name, eng, tt(dr, ar, br, ALU.mult))
            link(name, eng, tt(dr, dr, t1, ALU.subtract))
            link(name, eng, tt(t1, ai, br, ALU.mult))
            link(name, eng, tt(di, ar, bi, ALU.mult))
            if negate_im:
                return V.scalar_tensor_tensor(di, di, -1.0, t1, ALU.mult, ALU.subtract)
            return tt(di, di, t1, ALU.add)

        def s5_inputs(name, eng, V, i, tmp):
            pp = s5_zp(i)[1]
            g = slice(4 * i, 4 * i + 4)
            x = [y.rearrange("p (g h) -> p g h", h=16)[:, g, :].unsqueeze(2).to_broadcast([P, 4, 8, 16])
                 for y in s5_bt]
            a = [s5_pw[:, 7::-1][:, :, c, g].rearrange("p t g -> p g t").unsqueeze(3).to_broadcast([P, 4, 8, 16])
                 for c in range(2)]
            t1 = tmp[:, 0:512].rearrange("p (g t h) -> p g t h", g=4, h=16)
            return complex_mul(name, eng, V, pp[:, 0], pp[:, 1], x[0], x[1], a[0], a[1], t1)

        @block.gpsimd
        def _(pool):
            def pool_s5prep(s):
                pool.wait_ge(*at_("s5_bbar", s.i))
                for i in range(NI):
                    if not s5_on_pool(i):
                        continue
                    if i >= 2:
                        pool.wait_ge(*at_("aux_ready", s.pt[i - 2, 1]))
                    s5_inputs("pool", pool, pool, i, s5_tmp_pool).then_inc(*by("s5_pset", s.i, i))
                    pool.wait_ge(*at_("s5_pset", s.i, i))
                for c in range(2):
                    pool.wait_ge(s5_stored[c], 64 * NI // 2)
                pool.memset(s5_L, 0.0).then_inc(s5_l_zero, 1)

            pool.memset(ident[:, :], 0.0).then_inc(consts, 1)
            pool.memset(upper[:, :], 1.0).then_inc(consts, 1)
            pool.memset(below[:, :], 1.0).then_inc(consts, 1)
            pool.wait_ge(consts, 3)
            pool.affine_select(out=ident[:, :], in_=ident[:, :], compare_op=ALU.not_equal, fill=1.0, base=0,
                               pattern=[[-1, P]], channel_multiplier=1).then_inc(consts, 1)
            pool.affine_select(out=upper[:, :], in_=upper[:, :], compare_op=ALU.is_ge, fill=0.0, base=0,
                               pattern=[[1, 512]], channel_multiplier=-1).then_inc(consts, 1)
            pool.affine_select(out=below[:, :], in_=below[:, :], compare_op=ALU.is_gt, fill=0.0, base=0,
                               pattern=[[-1, P]], channel_multiplier=1).then_inc(consts, 1)
            pool.iota(junk[:, 1, :].bitcast(I32), [[1, 512]], base=-384, channel_multiplier=-1).then_inc(consts, 1)
            pool.wait_ge(consts, 7)
            pool.tensor_copy(bias_tile[:, :], junk[:, 1, :].bitcast(I32)).then_inc(consts, 1)
            pool.wait_ge(consts, 8)
            pool.affine_select(out=bias_tile[:, :], in_=bias_tile[:, :], compare_op=ALU.is_ge, fill=BIG, base=384,
                               pattern=[[-1, 512]], channel_multiplier=1).then_inc(consts, 1)
            for n in range(NUSED):
                pool.wait_ge(w_hi_done, n + 1)
                pool.tensor_tensor(w_lo[:, n % HL], raw[:, n % RAW], w_hi[:, n % HL].bitcast(F32),
                                   ALU.subtract).then_inc(w_lo_done, 1)
                for s in s5_preps:
                    if s.n == n - 1:
                        pool_s5prep(s)
                for k, s in enumerate(qk_chunks):
                    if s.n + 2 == n:
                        for m in range(s.T):
                            x = att[:, 12 + s.stage_at + m, :]
                            if k:
                                pool.wait_ge(*at_("summed", qk_chunks[k - 1].i, min(m, qk_chunks[k - 1].T - 1)))
                            pool.wait_ge(*at_("staged", s.i, m))
                            pool.tensor_tensor(sq[:, m, :], x, x, ALU.mult).then_inc(*by("q_squared", s.i, m))

        tri_at, TRI = [0, 512, 896, 1152], 1280
        workf = work[:, :, :].rearrange("p a b -> p (a b)")

        def tri(x, j=None):
            return x[:, 0:TRI] if j is None else x[:, tri_at[j]:tri_at[j] + SEQ - P * j]

        def sb_sp(hd, j=None):
            return tri(att[:, 16:21, :].rearrange("p a b -> p (a b)")[:, TRI * (hd % 2):TRI * (hd % 2) + TRI], j)

        def sb_lb(hd, j=None):
            x = workf[:, TRI:2 * TRI] if hd % 3 == 2 else \
                big[:, 16:21, :].rearrange("p a b -> p (a b)")[:, TRI * (hd % 3):TRI * (hd % 3) + TRI]
            return tri(x, j)

        def sb_z(hd, j=None):
            return tri(workf if hd % 2 else att[:, 21:24, :].rearrange("p a b -> p (a b)"), j)

        @block.scalar
        def _(act):
            def w_high(n):
                if n >= NUSED:
                    return
                act.wait_ge(raw_loaded[n % RAW], 32 * (n // RAW + 1))
                if n >= HL:
                    act.wait_ge(blocks, 4 * (n - HL + 1))
                parts = units[n]
                kn = parts[-1][1].stop
                nc.scalar.activation(w_hi[:, n % HL, 0:kn], raw[:, n % RAW, 0:kn], ACT.Copy).then_inc(w_hi_done, 1)

            def stage_qk(s, m, lim):
                act.wait_ge(blocks, lim)
                nc.scalar.activation(att[:, 12 + s.stage_at + m, :], G[:, m, :], ACT.Copy)\
                    .then_inc(*by("staged", s.i, m))

            def owed_copy(q, m):
                dst = big_mk if q.ev == "memkv" else q.to[:, q.dst:q.dst + 4, :]
                act.wait_ge(*at_("aux_ready", q.aux[m]))
                nc.scalar.activation(dst[:, :, m * P:(m + 1) * P],
                                     X[:, q.aux[m] % 4, :].rearrange("p (a b) -> p a b", b=P), ACT.Copy,
                                     scale=gain(q.name)).then_inc(*by("operand", q.i, m))

            def act_slot(s, t):
                if t >= s.slots:
                    return
                maps, T = 2 if s.akind == "A" else 1, len(s.steps)
                if 0 <= t - 2 < T:
                    hd, i = s.steps[t - 2]
                    nb = 2 if s.akind == "X" else i + 1
                    if hd and i == 0:
                        act.wait_ge(*at_("aux_ready", s.aux["pv", hd - 1]))
                    a = s.aux["pt", t - 2]
                    act.wait_ge(*at_("aux_ready", a))
                    nc.scalar.activation(att[:, 20:20 + nb, i * P:(i + 1) * P],
                                         X[:, a % 4, 0:nb * P].rearrange("p (a b) -> p a b", b=P),
                                         ACT.Copy).then_inc(*by("pt_copied", s.i, t - 2))
                if is_last(s, t - 3) and s.akind == "A":
                    hd = s.steps[t - 3][0]
                    if hd:
                        act.wait_ge(*at_("aux_ready", s.aux["ot", hd - 1]))
                    act.wait_ge(*at_("aux_ready", s.aux["pv", hd]))
                    nc.scalar.activation(junk[:, 0, :], X[:, s.aux["pv", hd] % 4, :], ACT.Square)\
                        .then_inc(*by("o_squared", s.i, hd))
                if t < T:
                    i = s.steps[t][1]
                    act.wait_ge(*at_("score", s.i, t))
                    for m in range(maps):
                        L = MEM if s.akind == "X" else P * (i + 1)
                        S = att[:, 16 + 2 * (t % 2) + m, 0:L]
                        src = X[:, s.aux["qk", t, 0] % 4, 0:L] if s.akind == "X" else S
                        c = 2 * (t % 2) + m
                        ins = nc.scalar.activation(S, src, ACT.Exp, bias=nmx[:, c:c + 1],
                                                   accum_out=rs[:, c:c + 1])
                    ins.then_inc(*by("exp_done", s.i, t))
                if t == s.slots - 1:
                    act.wait_ge(*at_("aux_ready", s.aux["ot" if s.akind == "A" else "pv", s.heads - 1]))

            def act_s5prep(s):
                act.wait_ge(*at_(*s.h))
                for c, name in enumerate(("a_lam_re", "a_lam_im")):
                    act.dma_start(s5_rows[:, c, :].rearrange("g (a p) -> g a p", a=2),
                                  w[name].rearrange("(a g) p -> g a p", a=2)).then_inc(s5_loaded, 16)
                    act.dma_start(s5_ldt[:, c:c + 1], w["a_log_dt"].rearrange("(a g o) -> a g o", a=2, o=1)[c])\
                       .then_inc(s5_loaded, 16)
                for c, name in enumerate(("a_c_re", "a_c_im")):
                    for k in range(4):
                        act.dma_start(s5_crow[c][:, k * P:(k + 1) * P].rearrange("p (a q) -> p a q", a=2),
                                      w[name].rearrange("(a k g) h q -> k (g h) a q", a=2, k=4)[k])\
                           .then_inc(s5_loaded, 16)
                for c, name in enumerate(("a_b_re", "a_b_im")):
                    for half in range(2):
                        act.dma_start(s5_b[c][64 * half:64 * half + 64].rearrange("p (g h) -> p g h", h=16),
                                      w[name].rearrange("(a g) p h -> a p g h", a=2)[half]).then_inc(s5_loaded, 16)
                act.wait_ge(*at_("s5_lam", s.i))
                link("act", act, nc.scalar.activation(s5_v(2), s5_v(2), ACT.Exp))
                nc.scalar.activation(s5_v(15), s5_v(2), ACT.Copy).then_inc(*by("s5_edt", s.i))
                act.wait_ge(*at_("s5_theta", s.i))
                link("act", act, nc.scalar.activation(s5_v(3), s5_v(3), ACT.Exp))
                nc.scalar.activation(s5_v(5), s5_v(5), ACT.Sin)
                nc.scalar.activation(s5_v(6), s5_v(6), ACT.Sin).then_inc(*by("s5_sin", s.i))
                for i in range(NI):
                    if i >= 2:
                        act.wait_ge(s5_stored[i % 2], 64 * (i // 2))
                    for c in range(2):
                        a = s.pt[i, c]
                        act.wait_ge(*at_("aux_ready", a))
                        nc.scalar.activation(s5_pst[i % 2][:, :, c, :], X[:, a % 4, :].rearrange("p (g n) -> p g n", g=4),
                                             ACT.Copy).then_inc(*by("s5_evac", s.i, i, "p", c))
                    for k in range(2):
                        a = s.kk[i, k]
                        act.wait_ge(*at_("aux_ready", a))
                        nc.scalar.activation(s5_kst[i % 2][:, 4 * k:4 * k + 4, :],
                                             X[0:16, a % 4, :].rearrange("p (g n) -> p g n", g=4),
                                             ACT.Copy).then_inc(*by("s5_evac", s.i, i, "k", k))
                    act.wait_ge(*at_("s5_evac", s.i, i, "k", 1))
                    act.dma_start(dP[:, i, :], s5_pst[i % 2].rearrange("p g c n -> p (g c n)"))\
                        .then_inc(s5_stored[i % 2], 16)
                    act.dma_start(dZ[:, i, :], s5_zp(i)[2]).then_inc(s5_stored[i % 2], 16)
                    for half in range(2):
                        act.dma_start(dK[32 * half + 4 * i:32 * half + 4 * i + 4].rearrange("g h n -> h g n"),
                                      s5_kst[i % 2][:, 4 * half:4 * half + 4, :]).then_inc(s5_stored[i % 2], 16)

            def s5_load(n):
                src, size = (dP[:, n, :], 1024) if n < NI else (dZ[:, n - NI, :], 1152)
                act.dma_start(s5_buf(n)[:, 0:size], src).then_inc(s5_op_loaded[n % S5B], 16)

            def act_s5_early():
                for c in range(2):
                    act.wait_ge(s5_stored[c], 64 * NI // 2)
                for n in range(S5B):
                    s5_load(n)
                act.wait_ge(s5_l_zero, 1)
                for t in range(8):
                    act.dma_start(s5_L[16 * t:16 * t + 16, :, 16 * t:P],
                                  dK[:, :, 0:P - 16 * t].rearrange("g h n -> h g n")).then_inc(s5_l_loaded, 16)

            def act_s5(s):
                act.wait_ge(s5_u_stored, 16 * 8)
                for t in range(8):
                    act.dma_start(s5_U[16 * t:16 * t + 16], dU[t].rearrange("g h j -> h g j")).then_inc(s5_u_loaded, 16)
                for i in range(NI):
                    act.wait_ge(*at_("aux_ready", s.v[i]))
                    s5_load(i + S5B)
                    nc.scalar.activation(s5_S[:, :, :, 4 * i:4 * i + 4].rearrange("p j c g -> p g c j"),
                                         X[:, s.v[i] % 4, :].rearrange("p (g c j) -> p g c j", g=4, c=2),
                                         ACT.Copy).then_inc(*by("s5_vdone", s.i, i))
                for i2 in range(2 * NI):
                    i, half = i2 // 2, i2 % 2
                    act.wait_ge(*at_("aux_ready", s.yy[i2]))
                    if half and i + S5B < NI:
                        s5_load(NI + i + S5B)
                    nc.scalar.activation(s5_U[:, 32 * half + 4 * i:32 * half + 4 * i + 4, :],
                                         X[:, s.yy[i2] % 4, 0:4 * NSUP].rearrange("p (g j) -> p g j", g=4), ACT.Copy)\
                        .then_inc(*by("s5_ydone", s.i, i2))
                act.wait_ge(*at_("s5_ydone", s.i, 2 * NI - 1))
                for t in range(8):
                    act.dma_start(dY[t].rearrange("g h j -> h g j"), s5_U[16 * t:16 * t + 16]).then_inc(s5_y_stored, 16)
                act.wait_ge(s5_y_stored, 16 * 8)
                for k in range(KT):
                    act.dma_start(s5_y[:, k, :].rearrange("p (t j) -> p t j", t=8),
                                  dY.rearrange("t (k g) h j -> (g h) k t j", k=8)[:, k]).then_inc(s5_y_loaded, 16)
                for k in range(KT):
                    act.wait_ge(*at_("s5_skip", s.i, k))
                    nc.scalar.activation(att[:, 16 + k, :].rearrange("p (j t) -> p j t", t=8),
                                         s5_y[:, k, :].rearrange("p (t j) -> p j t", t=8), ACT.Gelu_apprx_tanh)\
                        .then_inc(*by("s5_gelu", s.i, k))
                for k in range(KT):
                    act.wait_ge(*at_("s5_gelu", s.i, k))
                    nc.scalar.activation(u_hi[:, k, :], att[:, 16 + k, :], ACT.Copy)\
                        .then_inc(*by("u_hi_done", s.i, k))

            act.dma_start(mem_view, w["mem"].rearrange("(t p) n -> p t n", p=P)).then_inc(mem_loaded, 16)
            act.wait_ge(dconsts, 1)
            for dst, src in loads[1::2]:
                act.dma_start(dst, src).then_inc(par_loaded, 16)
            act.wait_ge(par_loaded, 16 * len(loads))
            act.wait_ge(dconsts, 4)
            act.wait_ge(consts, 9)
            nc.scalar.activation(lam_t[:, 2:4], lam_t[:, 0:2], ACT.Exp).then_inc(aconsts, 1)
            w_high(0)
            w_high(1)
            for s in plan:
                if s.kind == "norm":
                    src = mem_view if s.src == "mem" else h
                    if s.src == "mem":
                        act.wait_ge(mem_loaded, 16 * (mem_norms.index(s) + 1))
                    elif s.i == norms[1].i:
                        act.wait_ge(h_loaded, 32)
                    if norms.index(s) > 0 and not s.step:
                        prev = [x for x in norms[:norms.index(s)] if not x.step][-1]
                        act.wait_ge(*at_("xn_ready", prev.i, prev.T - 1))
                    for t in range(0 if s.step else s.T):
                        if s.src == "h" and s.h is not None:
                            act.wait_ge(*at_(*s.h[:-1], t))
                        if t or norms.index(s):
                            act.wait_ge(chain["act"], chained["act"])
                        nc.scalar.activation(junk[:, :, :].rearrange("p a b -> p (a b)"), src[:, t, :], ACT.Square,
                                             accum_out=ss[:, t:t + 1]).then_inc(*by("squared", s.i, t))
                        act.wait_ge(*at_("squared", s.i, t))
                    if s.n:
                        act.wait_ge(blocks, 4 * s.n)
                    act.wait_ge(dconsts, 5)
                    for k in range(KT):
                        act.wait_ge(*at_("aux_ready", s.aux[k]))
                        nc.scalar.activation(u_hi[:, k, 0:P * s.T], X[:, s.aux[k] % 4, 0:P * s.T], ACT.Copy,
                                             scale=gain(s.name, k)).then_inc(*by("u_hi_done", s.i, k))
                elif s.kind == "owed":
                    for m in range(s.owed.T):
                        owed_copy(s.owed, m)
                elif s.kind == "attend_rest":
                    for t in range(s.host_at, s.host.slots):
                        act_slot(s.host, t)
                elif s.kind == "chunk":
                    if s.y_before is not None and s.host is None and s.ev != "up":
                        act.wait_ge(*at_(*s.y_before))
                    if s.ev == "s5u" and s.dst == 0:
                        act_s5_early()
                    for u in range(s.nu):
                        n = s.n + u
                        if s.ev == "memkv" and u == 1:
                            for m in range(2):
                                stage_qk(s, m, 4 * n + 2 * m + 2)
                        for m in range(4):
                            if s.host is not None:
                                act_slot(s.host, s.host_at + 4 * u + m)
                            if s.owed is not None and u == 1 and m < s.owed.T:
                                owed_copy(s.owed, m)
                            if u == s.nu - 1:
                                if s.ev == "qk":
                                    stage_qk(s, m, 4 * n + m + 1)
                                elif s.ev == "s5u":
                                    act.wait_ge(blocks, 4 * n + m + 1)
                                    k = s.dst + m
                                    nc.scalar.activation(s5_u[:, k, :, :].rearrange("p t j -> p j t"),
                                                         G[:, m, :].rearrange("p (j t) -> p j t", t=8), ACT.Copy)\
                                        .then_inc(*by("operand", s.i, "v", m))
                                    act.wait_ge(*at_("operand", s.i, "v", m))
                                    act.dma_start(dU.rearrange("t (k g) h j -> (g h) k t j", k=8)[:, k],
                                                  s5_u[:, k]).then_inc(s5_u_stored, 16)
                                elif s.ev == "v":
                                    act.wait_ge(blocks, 4 * n + m + 1)
                                    nc.scalar.activation(att[:, s.dst + m * s.step, :], G[:, m, :], ACT.Copy)\
                                        .then_inc(*by("operand", s.i, "v", m))
                                elif s.ev == "memkv" and m >= 2:
                                    act.wait_ge(blocks, 4 * n + 2 * (m - 2) + 2)
                                    nc.scalar.activation(big_mv[:, m - 2, :], G[:, m, :], ACT.Copy)\
                                        .then_inc(*by("operand", s.i, "v", m))
                                elif s.ev == "silu" and m % 2:
                                    for k in (m - 1, m):
                                        act.wait_ge(blocks, 4 * n + k + 1)
                                        nc.scalar.activation(big[:, s.dst + k, :], G[:, k, :], ACT.Silu)\
                                            .then_inc(*by("gate", s.i, k))
                                elif s.ev == "conv_h":
                                    act.wait_ge(blocks, 4 * n + m + 1)
                                    nc.scalar.activation(big[:, 8 + m, :], G[:, m, :], ACT.Copy)\
                                        .then_inc(*by("gate", s.i, m))
                                elif s.ev == "conv_z":
                                    act.wait_ge(blocks, 4 * n + m + 1)
                                    act.wait_ge(*at_("conv", s.i - 2, m))
                                    nc.scalar.activation(big[:, 8 + m, :], G[:, m, :], ACT.Silu)\
                                        .then_inc(*by("gate", s.i, m))
                                elif s.ev == "up" and m < 2:
                                    act.wait_ge(*at_("conv", s.i, m))
                                    g = att[:, 4 * (s.c % 2) + m, :]
                                    nc.scalar.activation(g, g, ACT.Silu).then_inc(*by("gate", s.i, m))
                                elif s.ev == "glu":
                                    act.wait_ge(blocks, 4 * n + m + 1)
                                    nc.scalar.activation(att[:, 4 * (s.c % 2) + m, 0:256], G[:, m, 256:512],
                                                         ACT.Sigmoid).then_inc(*by("gate", s.i, m))
                        w_high(n + 2)
                elif s.kind == "attend":
                    for k in range(s.heads + 2):
                        if k < s.heads:
                            L = sb_lb(k)
                            if k >= 3:
                                act.wait_ge(*at_("aux_ready", s.aux["pv", k - 3]))
                            act.wait_ge(*at_("z", s.i, k, TT - 1))
                            link("act", act, nc.scalar.activation(L, sb_z(k), ACT.Abs))
                            link("act", act, nc.scalar.activation(L, L, ACT.Exp, scale=-1.0))
                        if k >= 2:
                            act.wait_ge(*at_("arg", s.i, k - 2, TT - 1))
                            e = sb_lb(k - 2)
                            nc.scalar.activation(e, e, ACT.Exp).then_inc(*by("exp_done", s.i, k - 2))
                        if k < s.heads:
                            nc.scalar.activation(L, L, ACT.Ln, bias=one_c).then_inc(*by("log_done", s.i, k))
                elif s.kind == "forget":
                    act.wait_ge(*at_("f_logit", s.i, TT - 1))
                    L3 = logt
                    link("act", act, nc.scalar.activation(L3, logf, ACT.Abs))
                    link("act", act, nc.scalar.activation(L3, L3, ACT.Exp, scale=-1.0))
                    nc.scalar.activation(L3, L3, ACT.Ln, bias=one_c).then_inc(*by("f_log", s.i))
                elif s.kind == "down":
                    act.wait_ge(*at_(*s.y))
                    act.wait_ge(blocks, 4 * s.n)

                    def y_high(g):
                        if g >= len(s.groups):
                            return
                        if g >= 2:
                            act.wait_ge(blocks, 4 * (s.n + 2 * (g - 1)))
                        for k in s.groups[g]:
                            nc.scalar.activation(u_hi[:, k % KT, :], big[:, k, :], ACT.Copy)\
                                .then_inc(*by("u_hi_done", s.i, k))
                    y_high(0)
                    y_high(1)
                    for g in range(len(s.groups)):
                        w_high(s.n + 2 * g + 2)
                        w_high(s.n + 2 * g + 3)
                        y_high(g + 2)
                elif s.kind == "s5prep":
                    act_s5prep(s)
                elif s.kind == "s5":
                    act_s5(s)

        @block.vector
        def _(dve):
            V = nc.vector
            V.memset(vec[:, 2, :], 0.0).then_inc(dconsts, 1)
            V.memset(eps_c, EPS).then_inc(dconsts, 1)
            V.memset(one_c, 1.0).then_inc(dconsts, 1)
            dve.wait_ge(par_loaded, 16 * len(loads))
            link("dve", dve, V.tensor_tensor(junk[:, 0, 256:320], junk[:, 0, 0:64], junk[:, 0, 64:128], ALU.mult))
            link("dve", dve, V.tensor_tensor(junk[:, 0, 320:384], junk[:, 0, 128:192], junk[:, 0, 192:256], ALU.mult))
            V.tensor_reduce(lam_t[:, 0:2], junk[:, 0, 256:384].rearrange("p (a b) -> p a b", a=2), AX_X,
                            ALU.add).then_inc(dconsts, 1)
            dve.wait_ge(*at_("aux_ready", gains.aux))
            V.tensor_copy(par[:, 0:pos], X[:, gains.aux % 4, 0:pos]).then_inc(*by("gains", 0))
            dve.wait_ge(*at_("gains", 0))
            dve.wait_ge(aconsts, 1)
            link("dve", dve, V.tensor_tensor(neg_lam, lam_t[:, 3:4], lam_t[:, 2:3], ALU.subtract))
            link("dve", dve, V.tensor_scalar(neg_lam, neg_lam, LAM_INIT, None, ALU.subtract))
            for name, f in (("aq", 64 ** -0.5), ("cq", P ** -0.5), ("exq", P ** -0.5), ("oxq", P ** -0.5),
                            ("sq", 64 ** -0.5), ("aout", 1.0 - LAM_INIT)):
                link("dve", dve, V.tensor_scalar(gain(name), gain(name), f, None, ALU.mult))
            V.memset(small[:, 60:61], 0.0).then_inc(dconsts, 1)

            def inverse_sqrt(y, v, t):
                link("dve", dve, V.tensor_scalar(t.bitcast(I32), v.bitcast(I32), 1, None, ALU.logical_shift_right))
                link("dve", dve, V.tensor_scalar(y.bitcast(I32), t.bitcast(I32), -1.0, float(0x5f3759df),
                                                 ALU.mult, ALU.add))
                for _ in range(3):
                    link("dve", dve, V.scalar_tensor_tensor(t, y, -0.5, y, ALU.mult, ALU.mult))
                    link("dve", dve, V.tensor_tensor(t, t, v, ALU.mult))
                    link("dve", dve, V.scalar_tensor_tensor(y, t, 1.5, y, ALU.add, ALU.mult))

            def inverse_rms(y, total, n, t):
                link("dve", dve, V.tensor_scalar(total, total, 1.0 / n, EPS, ALU.mult, ALU.add))
                inverse_sqrt(y, total, t)

            def finish_sum(q, m):
                nh = 512 // q.hd
                dve.wait_ge(*at_("q_squared", q.i, m))
                V.tensor_reduce(qk_ss[:, nh * m:nh * m + nh], sq[:, m, :].rearrange("p (a b) -> p a b", b=q.hd), AX_X,
                                ALU.add).then_inc(*by("summed", q.i, m))

            def finish_rms(q):
                dve.wait_ge(*at_("summed", q.i, q.T - 1))
                N = q.T * 512 // q.hd
                inverse_rms(qk_rstd[:, 0:N], qk_ss[:, 0:N], q.hd, qk_t[:, 0:N])

            def finish_scale(q, m):
                nh = 512 // q.hd
                x = att[:, 12 + q.stage_at + m, :].rearrange("p (a b) -> p a b", b=q.hd)
                V.tensor_tensor(x, x, qk_rstd[:, nh * m:nh * m + nh].unsqueeze(2).to_broadcast([P, nh, q.hd]),
                                ALU.mult).then_inc(*by("xn_ready", q.i, m))

            def conv(dst, src, cw, cb):
                link("dve", dve, V.tensor_scalar(dst, src, cw(2), cb, ALU.mult, ALU.add))
                link("dve", dve, V.scalar_tensor_tensor(dst[:, 1:SEQ], src[:, 0:SEQ - 1], cw(1), dst[:, 1:SEQ],
                                                        ALU.mult, ALU.add))
                return V.scalar_tensor_tensor(dst[:, 2:SEQ], src[:, 0:SEQ - 2], cw(0), dst[:, 2:SEQ],
                                              ALU.mult, ALU.add)

            def dve_slot(s, t):
                if t >= s.slots:
                    return
                T = len(s.steps)
                maps = 2 if s.akind == "A" else 1
                if t == 0:
                    dve.wait_ge(*at_(*s.gate))
                    if s.akind == "C":
                        dve.wait_ge(*at_(*s.operand))
                        V.tensor_scalar(row, cum, ident[0:C_HEADS, s.y0:s.y0 + 1], None, ALU.mult)\
                            .then_inc(*by("row_ready", s.i, 0))
                if t < T:
                    hd, i = s.steps[t]
                    head = s.y0 + hd
                    L = MEM if s.akind == "X" else P * (i + 1)
                    o = 2 * (t % 2)
                    if s.akind == "A" and i == 0:
                        link("dve", dve, V.tensor_scalar(junk[:, 1, :], bias_tile[:, :], 2.0 ** -(head + 1), None,
                                                         ALU.mult))
                    if t >= 2:
                        dve.wait_ge(*at_("aux_ready", s.aux["pt", t - 2]))
                    for m in range(maps):
                        a = s.aux["qk", t, m]
                        dve.wait_ge(*at_("aux_ready", a))
                        if s.akind == "X":
                            ins = V.tensor_reduce(mx[:, o:o + 1], X[:, a % 4, 0:L], AX_X, ALU.max)
                        else:
                            b = junk[:, 1, :] if s.akind == "A" else bias_tile[:, :]
                            ins = V.tensor_tensor_reduce(
                                out=att[:, 16 + o + m, 0:L], in0=X[:, a % 4, 0:L], in1=b[:, 384 - P * i:512],
                                scale=1.0, scalar=BIG, op0=ALU.add, op1=ALU.max, accum_out=mx[:, o + m:o + m + 1])
                    link("dve", dve, ins)
                    V.tensor_scalar(nmx[:, o:o + maps], mx[:, o:o + maps], -1.0, None, ALU.mult)\
                        .then_inc(*by("score", s.i, t))
                    if s.akind == "C" and i == TT - 1 and hd < s.heads - 1:
                        V.tensor_scalar(row, cum, ident[0:C_HEADS, head + 1:head + 2], None, ALU.mult)\
                            .then_inc(*by("row_ready", s.i, hd + 1))
                if 1 <= t <= T:
                    i = s.steps[t - 1][1]
                    L = MEM if s.akind == "X" else P * (i + 1)
                    o = 2 * ((t - 1) % 2)
                    S1, S2 = att[:, 16 + o, 0:L], att[:, 17 + o, 0:L]
                    dve.wait_ge(*at_("exp_done", s.i, t - 1))
                    link("dve", dve, V.reciprocal(rr[:, o:o + maps], rs[:, o:o + maps]))
                    if s.akind == "A":
                        link("dve", dve, V.tensor_tensor(rr[:, o + 1:o + 2], rr[:, o + 1:o + 2], neg_lam, ALU.mult))
                        link("dve", dve, V.tensor_scalar(S2, S2, rr[:, o + 1:o + 2], None, ALU.mult))
                        V.scalar_tensor_tensor(S1, S1, rr[:, o:o + 1], S2, ALU.mult, ALU.add)\
                            .then_inc(*by("p_ready", s.i, t - 1))
                    else:
                        V.tensor_scalar(S1, S1, rr[:, o:o + 1], None, ALU.mult)\
                            .then_inc(*by("p_ready", s.i, t - 1))
                if is_last(s, t - 3):
                    hd = s.steps[t - 3][0]
                    y = big[:, s.y0 + hd, :]
                    if s.akind == "A":
                        on = junk[:, 0, :].rearrange("p (a b) -> p a b", b=P)
                        dve.wait_ge(*at_("o_squared", s.i, hd))
                        link("dve", dve, V.tensor_reduce(oss, on, AX_X, ALU.add))
                        inverse_rms(orstd, oss, P, oln)
                        V.tensor_tensor(on, X[:, s.aux["pv", hd] % 4, :].rearrange("p (a b) -> p a b", b=P),
                                        orstd.unsqueeze(2).to_broadcast([P, TT, P]), ALU.mult)\
                            .then_inc(*by("on_ready", s.i, hd))
                    else:
                        a = s.aux["pv", hd]
                        dve.wait_ge(*at_("aux_ready", a))
                        V.tensor_tensor(y, X[:, a % 4, :], y, ALU.mult).then_inc(*by("y", s.i, hd))
                if is_last(s, t - 5) and s.akind == "A":
                    hd = s.steps[t - 5][0]
                    y = big[:, s.y0 + hd, :]
                    a = s.aux["ot", hd]
                    dve.wait_ge(*at_("aux_ready", a))
                    V.scalar_tensor_tensor(y, X[:, a % 4, :], gain("aout"), y, ALU.mult, ALU.mult)\
                        .then_inc(*by("y", s.i, hd))

            def dve_s5prep(s):
                v = s5_v
                tt, ts = V.tensor_tensor, V.tensor_scalar

                def do(ins):
                    link("dve", dve, ins)

                dve.wait_ge(s5_loaded, 16 * 16)
                V.tensor_copy(s5_rows[:, 2, :].rearrange("p (a b) -> p a b", a=2),
                              s5_ldt.unsqueeze(2).to_broadcast([NPAIR, 2, 64])).then_inc(*by("s5_dtrow", s.i))
                dve.wait_ge(*at_("aux_ready", s.at_lam))
                V.tensor_copy(att[:, 8, 0:96], X[:, s.at_lam % 4, 0:96]).then_inc(*by("s5_lam", s.i))
                for c in range(2):
                    dve.wait_ge(*at_("aux_ready", s.at_c[c]))
                    V.tensor_copy(s5_c[c], X[:, s.at_c[c] % 4, :]).then_inc(*by("s5_ct", s.i, c))
                dve.wait_ge(*at_("s5_edt", s.i))
                re, im, dt, er = v(0), v(1), v(2), v(3)
                do(tt(er, re, dt, ALU.mult))
                do(tt(v(4), im, dt, ALU.mult))
                do(ts(v(7), v(4), 0.15915494309189535, 12582912.0, ALU.mult, ALU.add))
                do(ts(v(7), v(7), 12582912.0, None, ALU.subtract))
                for part in (6.28125, 0.0019350051879882812, 3.0199159819e-07):
                    do(V.scalar_tensor_tensor(v(4), v(7), -part, v(4), ALU.mult, ALU.add))
                do(ts(v(5), v(4), 0.5, None, ALU.mult))
                do(ts(v(6), v(5), -1.0, None, ALU.mult))
                do(tt(v(6), v(5), v(6), ALU.max))
                ts(v(6), v(6), -1.0, 1.5707963267948966, ALU.mult, ALU.add).then_inc(*by("s5_theta", s.i))
                dve.wait_ge(*at_("s5_sin", s.i))
                s2, c2 = v(5), v(6)
                do(tt(v(8), s2, s2, ALU.mult))
                do(ts(v(8), v(8), -2.0, None, ALU.mult))
                do(tt(v(9), s2, c2, ALU.mult))
                do(ts(v(9), v(9), 2.0, None, ALU.mult))
                do(ts(v(10), er, 1.0, None, ALU.subtract))
                do(V.scalar_tensor_tensor(v(11), v(8), 1.0, v(10), ALU.add, ALU.mult))
                do(tt(v(11), v(11), v(8), ALU.add))
                do(tt(v(12), er, v(9), ALU.mult))
                do(ts(s5_pw[:, 1, 0, :], v(11), 1.0, None, ALU.add))
                do(V.tensor_copy(s5_pw[:, 1, 1, :], v(12)))
                do(V.memset(s5_pw[:, 0, 0, :], 1.0))
                do(V.memset(s5_pw[:, 0, 1, :], 0.0))
                do(tt(v(13), re, re, ALU.mult))
                do(tt(v(14), im, im, ALU.mult))
                do(tt(v(13), v(13), v(14), ALU.add))
                do(V.reciprocal(v(13), v(13)))
                do(tt(v(14), v(11), re, ALU.mult))
                do(tt(v(15), v(12), im, ALU.mult))
                do(tt(v(14), v(14), v(15), ALU.add))
                do(tt(v(16), v(14), v(13), ALU.mult))
                do(tt(v(14), v(12), re, ALU.mult))
                do(tt(v(15), v(11), im, ALU.mult))
                do(tt(v(14), v(14), v(15), ALU.subtract))
                do(tt(v(17), v(14), v(13), ALU.mult))
                for lo, n in ((1, 1), (2, 2), (4, 4)):
                    a = s5_pw[:, 1:n + 1, :, :]
                    d = s5_pw[:, lo + 1:lo + 1 + n, :, :]
                    b = s5_pw[:, lo:lo + 1, :, :]
                    bc = lambda c: b[:, :, c, :].to_broadcast([P, n, NPAIR])
                    t1 = s5_tmp[:, 0:n * NPAIR].rearrange("p (a b) -> p a b", a=n)
                    do(complex_mul("dve", dve, V, d[:, :, 0, :], d[:, :, 1, :], a[:, :, 0, :], a[:, :, 1, :], bc(0), bc(1), t1))
                for c in range(2):
                    do(V.tensor_copy(s5_coef[:, 0, c, :], s5_pw[:, 8, 0, :]))
                    do(ts(s5_coef[:, 1, c, :], s5_pw[:, 8, 1, :], 2.0 * c - 1.0, None, ALU.mult))
                h3 = lambda x: x.rearrange("p (g h) -> p g h", h=16)
                bf = lambda k: v(k).unsqueeze(2).to_broadcast([P, NPAIR, 16])
                complex_mul("dve", dve, V, h3(s5_bt[0]), h3(s5_bt[1]), h3(s5_b[0]), h3(s5_b[1]), bf(16), bf(17), h3(s5_tmp[:, 0:512]))\
                    .then_inc(*by("s5_bbar", s.i))
                dve.wait_ge(*at_("s5_bbar", s.i))
                for i in range(NI):
                    z = s5_zp(i)[0]
                    if not s5_on_pool(i):
                        dve.wait_ge(*at_("aux_ready", s.pt[i - 2, 1]))
                        do(s5_inputs("dve", dve, V, i, s5_tmp))
                    if i >= 2:
                        dve.wait_ge(s5_stored[i % 2], 64 * (i // 2))
                    g = slice(4 * i, 4 * i + 4)
                    x = [h3(y)[:, g, :].unsqueeze(2).to_broadcast([P, 4, 9, 16]) for y in s5_c]
                    a = [s5_pw[:, 0:9][:, :, c, g].rearrange("p t g -> p g t").unsqueeze(3).to_broadcast([P, 4, 9, 16])
                         for c in range(2)]
                    t1 = s5_tmp[:, 0:576].rearrange("p (g t h) -> p g t h", g=4, h=16)
                    complex_mul("dve", dve, V, z[:, 0], z[:, 1], x[0], x[1], a[0], a[1], t1, negate_im=True)\
                        .then_inc(*by("s5_set", s.i, i))
                    dve.wait_ge(*at_("s5_set", s.i, i))
                for c in range(2):
                    dve.wait_ge(s5_stored[c], 64 * NI // 2)

            def dve_s5(s):
                dve.wait_ge(*at_("s5_vdone", s.i, NI - 1))
                t1 = s5_buf2[:, 0:64].rearrange("p (c g) -> p c g", c=2)
                t2 = s5_buf2[:, 64:128].rearrange("p (c g) -> p c g", c=2)
                for j in range(1, NSUP):
                    last = s5_S[:, j - 1]
                    V.tensor_tensor(t1, last, s5_coef[:, 0], ALU.mult).then_inc(chain["dve"], 1)
                    V.tensor_tensor(t2, last[:, ::-1, :], s5_coef[:, 1], ALU.mult).then_inc(chain["dve"], 1)
                    chained["dve"] += 2
                    dve.wait_ge(chain["dve"], chained["dve"] - 1)
                    link("dve", dve, V.tensor_tensor(t1, t1, s5_S[:, j], ALU.add))
                    ins = V.tensor_tensor(s5_S[:, j], t1, t2, ALU.add)
                    if j < NSUP - 1:
                        link("dve", dve, ins)
                    else:
                        ins.then_inc(*by("s5_scanned", s.i))
                for k in range(KT):
                    dve.wait_ge(s5_y_loaded, 16 * KT)
                    V.scalar_tensor_tensor(s5_y[:, k, :], att[:, k, :], gain("d_skip", k), s5_y[:, k, :],
                                           ALU.mult, ALU.add).then_inc(*by("s5_skip", s.i, k))
                for k in range(KT):
                    dve.wait_ge(*at_("u_hi_done", s.i, k))
                    V.tensor_tensor(u_lo[:, k, :], att[:, 16 + k, :], u_hi[:, k, :].bitcast(F32), ALU.subtract)\
                        .then_inc(*by("u_ready", s.i, k))

            def dve_sb(s):
                link("dve", dve, V.tensor_scalar(bias_tile[:, :], upper[:, :], -BIG, BIG, ALU.mult, ALU.add))
                link("dve", dve, V.scalar_tensor_tensor(bias_tile[:, 0:P], ident[:, :], BIG, bias_tile[:, 0:P],
                                                        ALU.mult, ALU.add))
                for k in range(s.heads + 3):
                    if k < s.heads:
                        if k >= 2:
                            dve.wait_ge(*at_("sp", s.i, k - 2))
                        for j in range(TT):
                            a = s.aux["qk", k, j]
                            dve.wait_ge(*at_("aux_ready", a))
                            V.tensor_tensor(sb_z(k, j), X[:, a % 4, 0:SEQ - P * j], bias_tile[:, 0:SEQ - P * j],
                                            ALU.add).then_inc(*by("z", s.i, k, j))
                    if 2 <= k < s.heads + 2:
                        for j in range(TT):
                            e = sb_lb(k - 2, j)
                            dve.wait_ge(*at_("later", s.i, k - 2, j))
                            V.tensor_tensor(e, e, G[:, j, 0:SEQ - P * j], ALU.subtract)\
                                .then_inc(*by("arg", s.i, k - 2, j))
                    if 1 <= k <= s.heads:
                        z, L = sb_z(k - 1), sb_lb(k - 1)
                        dve.wait_ge(*at_("log_done", s.i, k - 1))
                        link("dve", dve, V.scalar_tensor_tensor(sb_sp(k - 1), z, 0.0, L, ALU.max, ALU.add))
                        V.scalar_tensor_tensor(L, z, 0.0, L, ALU.min, ALU.subtract).then_inc(*by("sp", s.i, k - 1))
                    if k >= 3:
                        a, r = s.aux["pv", k - 3], 64 * ((k - 3) % 2)
                        dve.wait_ge(*at_("aux_ready", a))
                        V.tensor_copy(big[r:r + 64, (k - 3) // 2, :], X[r:r + 64, a % 4, :])\
                            .then_inc(*by("y", s.i, k - 3))

            for s in plan:
                if s.kind == "norm":
                    src = mem_view if s.src == "mem" else h
                    if not s.step:
                        dve.wait_ge(*at_("squared", s.i, s.T - 1))
                        inverse_rms(rstd[:, 0:s.T], ss[:, 0:s.T], DM, lnv[:, 0:s.T])
                    for t in range(0 if s.step else s.T):
                        V.tensor_scalar(xn_view[:, t, :], src[:, t, :], rstd[:, t:t + 1], None, ALU.mult)\
                            .then_inc(*by("xn_ready", s.i, t))
                    for k in range(KT):
                        dve.wait_ge(*at_("u_hi_done", s.i, k))
                        V.scalar_tensor_tensor(u_lo[:, k, 0:P * s.T], X[:, s.aux[k] % 4, 0:P * s.T], gain(s.name, k),
                                               u_hi[:, k, 0:P * s.T].bitcast(F32), ALU.mult, ALU.subtract)\
                            .then_inc(*by("u_ready", s.i, k))
                elif s.kind == "owed":
                    for m in range(s.owed.T):
                        finish_sum(s.owed, m)
                    finish_rms(s.owed)
                    for m in range(s.owed.T):
                        finish_scale(s.owed, m)
                elif s.kind == "attend_rest":
                    for t in range(s.host_at, s.host.slots):
                        dve_slot(s.host, t)
                elif s.kind == "chunk":
                    n = s.n + s.nu - 1
                    for b in range(8):
                        m = b - 4
                        if s.host is not None:
                            dve_slot(s.host, s.host_at + b)
                        if s.owed is not None:
                            if b < 2:
                                finish_sum(s.owed, 2 * b)
                                finish_sum(s.owed, 2 * b + 1)
                            elif b == 2:
                                finish_rms(s.owed)
                            elif b < 5:
                                finish_scale(s.owed, 2 * b - 6)
                                finish_scale(s.owed, 2 * b - 5)
                        if m < 0:
                            continue
                        if s.ev == "conv_c":
                            dve.wait_ge(blocks, 4 * n + m + 1)
                            dve.wait_ge(*at_("gate", s.i - 1, m))
                            c = big[:, 8 + m, :]
                            link("dve", dve, V.tensor_tensor(c, G[:, m, :], c, ALU.mult))
                            conv(att[:, 12 + m, :], c, lambda j: gain(f"e_cw{j}", m), gain("e_cb", m))\
                                .then_inc(*by("conv", s.i, m))
                        elif s.ev == "conv_b":
                            dve.wait_ge(blocks, 4 * n + m + 1)
                            dve.wait_ge(*at_("conv", s.i - 1, m))
                            V.tensor_tensor(att[:, 12 + m, :], G[:, m, :], att[:, 12 + m, :], ALU.mult)\
                                .then_inc(*by("conv", s.i, m))
                        elif s.ev == "conv_z":
                            dve.wait_ge(*at_("gate", s.i, m))
                            dve.wait_ge(*at_("conv", s.i - 1, m))
                            V.tensor_tensor(big[:, 8 + m, :], att[:, 12 + m, :], big[:, 8 + m, :], ALU.mult)\
                                .then_inc(*by("y", s.i, m))
                        elif s.ev == "up" and m < 2:
                            dve.wait_ge(blocks, 4 * n + m + 1)
                            c = s.dst + m
                            conv(att[:, 4 * (s.c % 2) + m, :], G[:, m, :],
                                 lambda j: gain(f"f{s.layer}_cw{j}", c), gain(f"f{s.layer}_cb", c))\
                                .then_inc(*by("conv", s.i, m))
                        elif s.ev == "glu":
                            dve.wait_ge(*at_("gate", s.i, m))
                            hv = h[:, m, s.dst:s.dst + 256]
                            tmp = att[:, 4 * (s.c % 2) + m, 0:256]
                            link("dve", dve, V.tensor_tensor(tmp, G[:, m, 0:256], tmp, ALU.mult))
                            V.tensor_tensor(hv, hv, tmp, ALU.add).then_inc(*by("h_done", s.i, m))
                        elif s.ev == "up":
                            dve.wait_ge(blocks, 4 * n + m + 1)
                            dve.wait_ge(*at_("gate", s.i, m - 2))
                            V.tensor_tensor(big[:, s.dst + m - 2, :], G[:, m, :], att[:, 4 * (s.c % 2) + m - 2, :],
                                            ALU.mult).then_inc(*by("y", s.i, m))
                elif s.kind == "attend":
                    dve_sb(s)
                elif s.kind == "forget":
                    lf = logf.rearrange("p (t n) -> p t n", t=TT)
                    for m in range(TT):
                        dve.wait_ge(*at_("aux_ready", s.aux[m]))
                        V.tensor_tensor(lf[:, m, :], X[:, s.aux[m] % 4, 0:C_HEADS], f_bias[:, :], ALU.add)\
                            .then_inc(*by("f_logit", s.i, m))
                    dve.wait_ge(*at_("f_log", s.i))
                    V.scalar_tensor_tensor(logf, logf, 0.0, logt, ALU.min, ALU.subtract)\
                        .then_inc(*by("log_f", s.i))
                    dve.wait_ge(*at_("aux_ready", s.aux_cum))
                    V.tensor_scalar(cum, X[0:C_HEADS, s.aux_cum % 4, :], -1.0, None, ALU.mult)\
                        .then_inc(*by("cum_done", s.i))
                    for o in range(0, 512, 512):
                        link("dve", dve, V.tensor_scalar(bias_tile[:, :], bias_tile[:, :], -1.0e30, 1.0e30, ALU.is_lt,
                                                         ALU.mult))
                        link("dve", dve, V.tensor_scalar(bias_tile[:, :], bias_tile[:, :], -3.0e8, None, ALU.mult))
                elif s.kind == "down":
                    for g in range(len(s.groups)):
                        for k in s.groups[g]:
                            dve.wait_ge(*at_("u_hi_done", s.i, k))
                            V.tensor_tensor(u_lo[:, k % KT, :], big[:, k, :], u_hi[:, k % KT, :].bitcast(F32),
                                            ALU.subtract).then_inc(*by("u_ready", s.i, k))
                    for col in range(2):
                        n = s.n + 2 * (len(s.groups) - 1) + col
                        for m in range(4):
                            dve.wait_ge(blocks, 4 * n + m + 1)
                            bank = G[:, m, :] if col == 0 else X[:, s.aux[m] % 4, :]
                            hv = h[:, m, 512 * col:512 * col + 512]
                            V.tensor_tensor(hv, bank, hv, ALU.add).then_inc(*by("h_done", s.i, col, m))
                elif s.kind == "s5prep":
                    dve_s5prep(s)
                elif s.kind == "s5":
                    dve_s5(s)

        @block.tensor
        def _(pe):
            def bank(a):
                if a >= 4:
                    pe.wait_ge(*at_(*freed[a - 4]))
                return X[:, a % 4, :]

            def three(out, lhs, rhs, start, stop):
                (lh, ll), (rh, rl) = lhs, rhs
                pe.matmul(out, lh, rh, start=start, stop=False)
                pe.matmul(out, lh, rl, start=False, stop=False)
                return pe.matmul(out, ll, rh, start=False, stop=stop)

            def owed(q, m):
                pe.wait_ge(*at_("xn_ready", q.i, m))
                b = bank(q.aux[m])
                for k in range(4):
                    ins = pe.transpose(b[:, k * P:(k + 1) * P], att[:, 12 + q.stage_at + m, k * P:(k + 1) * P],
                                       ident[:, :])
                ins.then_inc(*by("aux_ready", q.aux[m]))

            def pe_slot(s, t):
                if t >= s.slots:
                    return
                T = len(s.steps)
                if t == 0:
                    pe.wait_ge(*at_(*s.operand))
                if is_last(s, t - 5) and s.akind == "A":
                    hd = s.steps[t - 5][0]
                    pe.wait_ge(*at_("on_ready", s.i, hd))
                    b = bank(s.aux["ot", hd])
                    for k in range(TT):
                        ins = pe.transpose(b[:, k * P:(k + 1) * P], junk[:, 0, k * P:(k + 1) * P], ident[:, :])
                    ins.then_inc(*by("aux_ready", s.aux["ot", hd]))
                if is_last(s, t - 3):
                    hd = s.steps[t - 3][0]
                    pe.wait_ge(*at_("pt_copied", s.i, t - 3))
                    b = bank(s.aux["pv", hd])
                    v = slice(hd * P, (hd + 1) * P)
                    if s.akind == "A":
                        for i in range(TT):
                            for j in range(i + 1):
                                ins = pe.matmul(b[:, i * P:(i + 1) * P], att[:, 20 + j, i * P:(i + 1) * P],
                                                att[:, 8 + j, v], start=j == 0, stop=j == i)
                    elif s.akind == "C":
                        for j in range(TT):
                            ins = pe.matmul(b[:, P * j:SEQ], att[:, 8 + j, v], att[:, 20 + j, P * j:SEQ],
                                            start=j == 0, stop=j == TT - 1)
                    else:
                        for j in range(2):
                            ins = pe.matmul(b, big_mv[:, j, v], att[:, 20 + j, :], start=j == 0, stop=j == 1)
                    ins.then_inc(*by("aux_ready", s.aux["pv", hd]))
                if 0 <= t - 2 < T:
                    i = s.steps[t - 2][1]
                    pe.wait_ge(*at_("p_ready", s.i, t - 2))
                    b = bank(s.aux["pt", t - 2])
                    S = att[:, 16 + 2 * (t % 2), :]
                    for j in range(2 if s.akind == "X" else i + 1):
                        ins = pe.transpose(b[:, j * P:(j + 1) * P], S[:, j * P:(j + 1) * P], ident[:, :])
                    ins.then_inc(*by("aux_ready", s.aux["pt", t - 2]))
                if t < T:
                    hd, i = s.steps[t]
                    q = att[:, hd, i * P:(i + 1) * P]
                    if s.akind == "C" and i == 0:
                        pe.wait_ge(*at_("row_ready", s.i, hd))
                    for m in range(2 if s.akind == "A" else 1):
                        b = bank(s.aux["qk", t, m])
                        L = P * (i + 1)
                        if s.akind == "X":
                            ins = pe.matmul(b[:, 0:MEM], q, big_mk[:, hd, :], start=True, stop=True)
                        elif s.akind == "C":
                            pe.matmul(b[:, 0:L], q, att[:, 4 + hd, 0:L], start=True, stop=False)
                            ins = pe.matmul(b[:, 0:L], ones[0:C_HEADS, :], row[:, 0:L], start=False, stop=True)
                        else:
                            r = slice(64 * m, 64 * m + 64)
                            ins = pe.matmul(b[:, 0:L], q[r, :], att[r, 4 + hd, 0:L], start=True, stop=True)
                        ins.then_inc(*by("aux_ready", s.aux["qk", t, m]))

            pe.wait_ge(consts, 9)
            pe.wait_ge(par_loaded, 16 * len(loads))
            for k in range(3):
                ins = pe.transpose(bank(gains.aux)[:, k * P:(k + 1) * P], vec[:, k, :], ident[:, :])
            ins.then_inc(*by("aux_ready", gains.aux))
            for s in plan:
                if s.kind == "norm":
                    for t in range(0 if s.step else s.T):
                        pe.wait_ge(*at_("xn_ready", s.i, t))
                    for k in range(KT):
                        b = bank(s.aux[k])
                        for t in range(s.T):
                            ins = pe.transpose(b[:, t * P:(t + 1) * P], xn_view[:, t, k * P:(k + 1) * P], ident[:, :])
                        ins.then_inc(*by("aux_ready", s.aux[k]))
                elif s.kind == "owed":
                    for m in range(s.owed.T):
                        owed(s.owed, m)
                elif s.kind == "attend_rest":
                    for t in range(s.host_at, s.host.slots):
                        pe_slot(s.host, t)
                elif s.kind == "chunk":
                    for u in range(s.nu):
                        n = s.n + u
                        pe.wait_ge(w_lo_done, n + 1)
                        for j in range(4):
                            if s.host is not None:
                                pe_slot(s.host, s.host_at + 4 * u + j)
                            m = j
                            ks = range(4)
                            if s.wtype == "mem":
                                m, ks = 2 * (u // 2) + j // 2, range(2 * (j % 2), 2 * (j % 2) + 2)
                            first = u == 0 if s.wtype != "mem" else (u % 2 == 0 and j % 2 == 0)
                            if first and s.c:
                                pe.wait_ge(*at_(*gfreed[m][s.c - 1]))
                            for k in ks:
                                K = 4 * (u % 2) + k
                                if (s.wtype != "mem" and m == 0) or (s.wtype == "mem" and m == 0):
                                    pe.wait_ge(*at_(*s.kt_ready[K]))
                                W = w_hi[:, n % HL, k, :], w_lo[:, n % HL, k, :]
                                if s.wtype == "T":
                                    c = slice(m * P, (m + 1) * P)
                                    ins = three(G[:, m, :], (W[0][:, c], W[1][:, c]), (u_hi[:, K, :], u_lo[:, K, :]),
                                                K == 0, K == KT - 1)
                                else:
                                    tok = m % 2 if s.wtype == "mem" else m
                                    c = slice(tok * P, (tok + 1) * P)
                                    ins = three(G[:, m, :], (u_hi[:, K, c], u_lo[:, K, c]), W, K == 0, K == KT - 1)
                            ins.then_inc(blocks, 1)
                            if s.owed is not None and u == 1 and j < s.owed.T:
                                owed(s.owed, j)
                elif s.kind == "down":
                    for g, ks in enumerate(s.groups):
                        for col in range(2):
                            n = s.n + 2 * g + col
                            pe.wait_ge(w_lo_done, n + 1)
                            for m in range(4):
                                if g == 0:
                                    if col == 0:
                                        pe.wait_ge(*at_(*gfreed[m][s.c - 1]))
                                    else:
                                        bank(s.aux[m])
                                out_bank = G[:, m, :] if col == 0 else X[:, s.aux[m] % 4, :]
                                for k in ks:
                                    if m == 0 and col == 0:
                                        pe.wait_ge(*at_("u_ready", s.i, k))
                                    c = slice(m * P, (m + 1) * P)
                                    ins = three(out_bank, (u_hi[:, k % KT, c], u_lo[:, k % KT, c]),
                                                (w_hi[:, n % HL, k % 4, :], w_lo[:, n % HL, k % 4, :]),
                                                k == 0, k == s.kt - 1)
                                ins.then_inc(blocks, 1)
                elif s.kind == "forget":
                    lf = logf.rearrange("p (t n) -> p t n", t=TT)
                    wc = wcf.rearrange("p (k n) -> p k n", k=KT)
                    for k in range(KT):
                        pe.wait_ge(*at_(*s.kt_ready[k]))
                    for m in range(TT):
                        b = bank(s.aux[m])[:, 0:C_HEADS]
                        for k in range(KT):
                            c = slice(m * P, (m + 1) * P)
                            pe.matmul(b, u_hi[:, k, c].bitcast(F32), wc[:, k, :], start=k == 0, stop=False)
                            ins = pe.matmul(b, u_lo[:, k, c].bitcast(F32), wc[:, k, :], start=False, stop=k == KT - 1)
                        ins.then_inc(*by("aux_ready", s.aux[m]))
                    pe.wait_ge(*at_("log_f", s.i))
                    b = bank(s.aux_cum)
                    for j in range(TT):
                        ins = pe.matmul(b[0:C_HEADS, P * j:SEQ], lf[:, j, :], upper[:, 0:SEQ - P * j],
                                        start=j == 0, stop=j == TT - 1)
                    ins.then_inc(*by("aux_ready", s.aux_cum))
                elif s.kind == "attend":
                    pe.wait_ge(*at_(*s.operand))
                    vv = att[:, 0:8, :].rearrange("p (t a) n -> p t (a n)", a=2)
                    for k in range(-1, s.heads + 2):
                        if k + 1 < s.heads:
                            hd = k + 1
                            r = slice(64 * (hd % 2), 64 * (hd % 2) + 64)
                            for j in range(TT):
                                b = bank(s.aux["qk", hd, j])
                                pe.matmul(b[:, 0:SEQ - P * j], big[r, 8 + hd // 2, j * P:(j + 1) * P],
                                          att[r, 8 + hd // 2, j * P:SEQ], start=True, stop=True)\
                                    .then_inc(*by("aux_ready", s.aux["qk", hd, j]))
                        if 1 <= k <= s.heads:
                            g = k - 1
                            pe.wait_ge(*at_("sp", s.i, g))
                            for j in range(TT):
                                pe.wait_ge(*at_(*(("arg", s.i, g - 1, j) if g else s.gfreed[j])))
                                b = G[:, j, :]
                                ins = pe.matmul(b[:, 0:SEQ - P * j], below[:, :], sb_sp(g, j), start=True,
                                                stop=j == TT - 1)
                                for i in range(j + 1, TT):
                                    ins = pe.matmul(b[:, P * (i - j):SEQ - P * j], ones[:, :], sb_sp(g, i),
                                                    start=False, stop=i == TT - 1)
                                ins.then_inc(*by("later", s.i, g, j))
                        if k >= 2:
                            g = k - 2
                            pe.wait_ge(*at_("exp_done", s.i, g))
                            b = bank(s.aux["pv", g])
                            r = slice(64 * (g % 2), 64 * (g % 2) + 64)
                            for j in range(TT):
                                ins = pe.matmul(b[r, P * j:SEQ], vv[:, j, 64 * g:64 * g + 64], sb_lb(g, j),
                                                start=j == 0, stop=j == TT - 1)
                            ins.then_inc(*by("aux_ready", s.aux["pv", g]))
                elif s.kind == "s5prep":
                    pe.wait_ge(*at_("s5_dtrow", s.i))
                    b = bank(s.at_lam)
                    for c in range(3):
                        ins = pe.transpose(b[:, 32 * c:32 * c + 32], s5_rows[:, c, :], ident[0:NPAIR, 0:NPAIR])
                    ins.then_inc(*by("aux_ready", s.at_lam))
                    for c in range(2):
                        b = bank(s.at_c[c])
                        for k in range(4):
                            ins = pe.transpose(b[:, k * P:(k + 1) * P], s5_crow[c][:, k * P:(k + 1) * P], ident[:, :])
                        ins.then_inc(*by("aux_ready", s.at_c[c]))
                    for i in range(NI):
                        z, pp, _ = s5_zp(i)
                        pe.wait_ge(*at_("s5_pset" if s5_on_pool(i) else "s5_set", s.i, i))
                        for c in range(2):
                            b = bank(s.pt[i, c])
                            for g in range(4):
                                ins = pe.transpose(b[:, g * P:(g + 1) * P],
                                                   pp[:, c, g].rearrange("p t h -> p (t h)"), ident[:, :])
                            ins.then_inc(*by("aux_ready", s.pt[i, c]))
                        pe.wait_ge(*at_("s5_set", s.i, i))
                        for k in range(2):
                            b = bank(s.kk[i, k])
                            for q in range(4):
                                g, r = q, slice(64 * k, 64 * k + 64)
                                for c in range(2):
                                    ins = pe.matmul(b[0:16, q * P:(q + 1) * P],
                                                    s5_bt[c][r, 64 * i + 16 * g:64 * i + 16 * g + 16],
                                                    z[r, c, g, 0:8].rearrange("p t h -> p (t h)"),
                                                    start=c == 0, stop=c == 1)
                            ins.then_inc(*by("aux_ready", s.kk[i, k]))
                elif s.kind == "s5":
                    pe.wait_ge(s5_u_loaded, 16 * 8)
                    for i in range(NI):
                        pe.wait_ge(s5_op_loaded[i % S5B], 16 * (i // S5B + 1))
                        b = bank(s.v[i])
                        op = s5_buf(i)[:, 0:1024].rearrange("p (g c n) -> p g c n", g=4, c=2)
                        for g in range(4):
                            for half in range(2):
                                r = slice(64 * half, 64 * half + 64)
                                for c in range(2):
                                    o = 64 * (2 * g + c)
                                    ins = pe.matmul(b[r, o:o + NSUP], op[:, g, c, r], s5_U[:, 32 * half + 4 * i + g, :],
                                                    start=True, stop=True)
                        ins.then_inc(*by("aux_ready", s.v[i]))
                    pe.wait_ge(s5_l_loaded, 16 * 8)
                    pe.wait_ge(*at_("s5_scanned", s.i))
                    for i in range(NI):
                        pe.wait_ge(s5_op_loaded[(NI + i) % S5B], 16 * ((NI + i) // S5B + 1))
                        op = s5_buf(NI + i).rearrange("p (c g n) -> p c g n", c=2, g=4)
                        for q in range(8):
                            g, r = q % 4, slice(64 * (q // 4), 64 * (q // 4) + 64)
                            o, k = NSUP * (q % 4), 32 * (q // 4) + 4 * i + q % 4
                            if q % 4 == 0:
                                b = bank(s.yy[2 * i + q // 4])
                            pe.matmul(b[:, o:o + NSUP], s5_L[:, k, :], s5_U[:, k, :],
                                      start=True, stop=False)
                            for c in range(2):
                                ins = pe.matmul(b[:, o + 1:o + NSUP], op[r, c, g, 16:144],
                                                s5_S[r, 0:NSUP - 1, c, 4 * i + g], start=False, stop=c == 1)
                            if q % 4 == 3:
                                ins.then_inc(*by("aux_ready", s.yy[2 * i + q // 4]))


def kernel(**inputs):
    import numpy as _np
    import concourse.bacc as _bacc
    from concourse import mybir as _mybir
    from concourse.bass_utils import run_bass_kernel_spmd as _run

    nc = _bacc.Bacc("TRN2", target_bir_lowering=False, num_devices=1)
    arrays, args = {}, {}
    for name, value in inputs.items():
        a = _np.ascontiguousarray(value)
        arrays[f"in_{name}"] = a
        ap = nc.dram_tensor(f"in_{name}", a.shape, _mybir.dt.from_np(a.dtype), kind="ExternalInput").ap()
        key = name[:-2] if name.endswith("_2") else name
        keep = name in ("ffn_norm_2", "ffn_w_up_2", "ffn_conv_w_2", "ffn_conv_b_2", "ffn_w_down_2")
        args[key] = ap[0] if a.shape[0] == 1 and not keep else ap
    out = nc.dram_tensor("out_0", (1, SEQ, DM), F32, kind="ExternalOutput").ap()
    build(nc, args, out[0])
    r = _run(nc, [arrays], core_ids=[0])
    return r.results[0]["out_0"]
```
